# Optimizing a Trainium2 kernel written in Bass

```python
import math
import jax, jax.numpy as jnp
from jax import lax
import numpy as np

D_MODEL = 1024
BATCH = 1
SEQ = 128
DEPTH = 2
DEC_BATCH = 1
DEC_SEQ = 256
PAST_LEN = 128

GRID_W = 64
N_EVEN = (DEPTH + 1) // 2
N_ODD = DEPTH // 2
D_A = D_MODEL // 2
D_B = D_MODEL - D_A
A_HEADS = 4
A_DK = D_A // A_HEADS
A_DV = D_A // A_HEADS
B_HEADS = 8
B_DH = D_B // B_HEADS
NA_ROWS = 8
NA_COLS = 16
CHUNK = 32
Q_BLOCK = 128
CONV_W = 3
D_FF = ((8 * D_MODEL // 3 + 127) // 128) * 128
N_MOD = 9
AB_IN = 5 * D_A + 3 * D_B
EPS = 1e-6
LB_MAX = 1.0 - 1e-4

kernel_name = "hybrid_hgrn2_natten_shortconv_diffusion_step"

def rmsnorm(x, g):
    xf = x.astype(jnp.float32)
    y = xf * lax.rsqrt(jnp.mean(xf * xf, axis=-1, keepdims=True) + EPS)
    return (y * g.astype(jnp.float32)).astype(x.dtype)

def adaln(cond, w, b):
    return (jax.nn.silu(cond) @ w + b)[:, None, :]

def mod_chunk(mod, i):
    return mod[..., i * D_MODEL:(i + 1) * D_MODEL]

def pre_norm(x, mod, j, g):
    return rmsnorm(x, g) * (1 + mod_chunk(mod, 3 * j + 1)) + mod_chunk(mod, 3 * j)

def post_residual(x, out, mod, j, g, w):
    return x + w * mod_chunk(mod, 3 * j + 2) * rmsnorm(out, g)

def swiglu(h, w_in, w_out):
    gate, up = jnp.split(h @ w_in, 2, axis=-1)
    return (jax.nn.silu(gate) * up) @ w_out

def hgrn2_lower_bounds(a_lb):
    p = jax.nn.softmax(a_lb.astype(jnp.float32), axis=0)
    return jnp.clip(jnp.cumsum(p, axis=0) - p[0], 0.0, LB_MAX)

def hgrn2_forget(z, lb):
    f = lb + (1.0 - lb) * jax.nn.sigmoid(z)
    log_f = jnp.maximum(jnp.log1p(-lb) + jax.nn.log_sigmoid(z), jnp.log(jnp.maximum(f, 1e-30)))
    k = (1.0 - lb) * jax.nn.sigmoid(-z)
    return log_f, k

def chunk_scan(q, k, v, log_f, s0):
    Bn, L, H, _ = q.shape
    n = L // CHUNK

    def chunks(t):
        return t.reshape(Bn, n, CHUNK, H, t.shape[-1]).transpose(1, 0, 3, 2, 4)

    causal = jnp.tril(jnp.ones((CHUNK, CHUNK), dtype=bool))[:, :, None]

    def step(S, blk):
        qc, kc, vc, gc = blk
        b = jnp.cumsum(gc, axis=2)
        diff = jnp.where(causal, b[:, :, :, None, :] - b[:, :, None, :, :], -jnp.inf)
        decay = jnp.exp(diff)
        att = jnp.einsum('bhtk,bhsk,bhtsk->bhts', qc, kc, decay)
        o = jnp.einsum('bhts,bhsv->bhtv', att, vc) + jnp.einsum('bhtk,bhkv->bhtv', qc * jnp.exp(b), S)
        b_end = b[:, :, -1:, :]
        S = (jnp.exp(b_end[:, :, 0, :])[..., None] * S
             + jnp.einsum('bhsk,bhsv->bhkv', kc * jnp.exp(b_end - b), vc))
        return S, o

    S, o = lax.scan(step, s0, (chunks(q), chunks(k), chunks(v), chunks(log_f)))
    return o.transpose(1, 0, 3, 2, 4).reshape(Bn, L, H, -1), S

def hgrn2_mixer(a_q, a_ffw, a_fbw, a_i, a_g, lb, gnorm, s0):
    Bn, L, _ = a_q.shape

    def heads(t):
        return t.astype(jnp.float32).reshape(Bn, L, A_HEADS, -1)

    q, v = heads(a_q), heads(a_i)
    logf_f, k_f = hgrn2_forget(heads(a_ffw), lb[0].reshape(A_HEADS, A_DK))
    logf_b, k_b = hgrn2_forget(heads(a_fbw), lb[1].reshape(A_HEADS, A_DK))
    o_f, s_f = chunk_scan(q, k_f, v, logf_f, s0[:, 0])

    def flip(t):
        return jnp.flip(t, axis=1)

    o_b, s_b = chunk_scan(flip(q), flip(k_b), flip(v), flip(logf_b), s0[:, 1])
    o = rmsnorm(o_f + flip(o_b), gnorm).reshape(Bn, L, D_A)
    o = o * jax.nn.silu(a_g.astype(jnp.float32))
    return o.astype(a_q.dtype), jnp.stack([s_f, s_b], axis=1)

def na_heads(t):
    Bn, L, _ = t.shape
    return t.reshape(Bn, L, B_HEADS, B_DH).transpose(0, 2, 1, 3)

def context_attention(q, k, v):
    Bn, H, L, dh = q.shape
    nb = L // Q_BLOCK
    scale = 1.0 / math.sqrt(dh)
    qb = q.reshape(Bn, H, nb, Q_BLOCK, dh).transpose(2, 0, 1, 3, 4)

    def blk(qi):
        s = jnp.einsum('bhqd,bhkd->bhqk', qi, k).astype(jnp.float32) * scale
        p = jax.nn.softmax(s, axis=-1).astype(v.dtype)
        return jnp.einsum('bhqk,bhkd->bhqd', p, v)

    o = lax.map(blk, qb)
    return o.transpose(1, 2, 0, 3, 4).reshape(Bn, H, L, dh)

def neighbourhood_attention(q, k, v, ck, cv, rpb):
    Bn, H, L, dh = q.shape
    rows = L // GRID_W
    wr = min(NA_ROWS, rows)
    scale = 1.0 / math.sqrt(dh)
    r = jnp.arange(rows)
    key_rows = jnp.clip(r - wr // 2, 0, rows - wr)[:, None] + jnp.arange(wr)[None, :]
    col = jnp.arange(GRID_W)
    c0 = jnp.clip(col - NA_COLS // 2, 0, GRID_W - NA_COLS)
    col_ok = (col[None, :] >= c0[:, None]) & (col[None, :] < c0[:, None] + NA_COLS)
    qg = q.reshape(Bn, H, rows, GRID_W, dh)
    kg = k.reshape(Bn, H, rows, GRID_W, dh)[:, :, key_rows]
    vg = v.reshape(Bn, H, rows, GRID_W, dh)[:, :, key_rows]
    s_loc = jnp.einsum('bhrqd,bhrjkd->bhrqjk', qg, kg).astype(jnp.float32) * scale
    r_idx = (key_rows - r[:, None] + NA_ROWS - 1)[:, None, :, None]
    c_idx = jnp.clip(col[None, :] - col[:, None], -(NA_COLS - 1), NA_COLS - 1) + NA_COLS - 1
    bias = rpb.astype(jnp.float32)[:, r_idx, c_idx[None, :, None, :]]
    s_loc = jnp.where(col_ok[:, None, :], s_loc + bias[None], -jnp.inf)
    s_loc = s_loc.reshape(Bn, H, rows, GRID_W, wr * GRID_W)
    s_ctx = jnp.einsum('bhrqd,bhcd->bhrqc', qg, ck).astype(jnp.float32) * scale
    p = jax.nn.softmax(jnp.concatenate([s_loc, s_ctx], axis=-1), axis=-1)
    p_loc = p[..., :wr * GRID_W].reshape(Bn, H, rows, GRID_W, wr, GRID_W).astype(v.dtype)
    p_ctx = p[..., wr * GRID_W:].astype(v.dtype)
    o = (jnp.einsum('bhrqjk,bhrjkd->bhrqd', p_loc, vg)
         + jnp.einsum('bhrqc,bhcd->bhrqd', p_ctx, cv))
    return o.reshape(Bn, H, L, dh)

def split_even(p):
    idx = [D_A, 2 * D_A, 3 * D_A, 4 * D_A, 5 * D_A, 5 * D_A + D_B, 5 * D_A + 2 * D_B]
    return jnp.split(p, idx, axis=-1)

def even_mixer_context(h, w_in, w_out, lb, gnorm):
    Bn, L, _ = h.shape
    a_q, a_ff, a_fb, a_i, a_g, b_q, b_k, b_v = split_even(h @ w_in)
    s0 = jnp.zeros((Bn, 2, A_HEADS, A_DK, A_DV), jnp.float32)
    o_a, s_fin = hgrn2_mixer(a_q, a_ff, a_fb, a_i, a_g, lb, gnorm, s0)
    q, k, v = na_heads(b_q), na_heads(b_k), na_heads(b_v)
    o_b = context_attention(q, k, v).transpose(0, 2, 1, 3).reshape(Bn, L, D_B)
    out = jnp.concatenate([o_a, o_b], axis=-1) @ w_out
    return out, s_fin, k, v

def even_mixer_latent(h, w_in, w_out, lb, gnorm, rpb, s_ctx, k_ctx, v_ctx):
    Bn, L, _ = h.shape
    a_q, a_ff, a_fb, a_i, a_g, b_q, b_k, b_v = split_even(h @ w_in)
    o_a, _ = hgrn2_mixer(a_q, a_ff, a_fb, a_i, a_g, lb, gnorm, s_ctx.astype(jnp.float32))
    o_b = neighbourhood_attention(na_heads(b_q), na_heads(b_k), na_heads(b_v), k_ctx, v_ctx, rpb)
    o_b = o_b.transpose(0, 2, 1, 3).reshape(Bn, L, D_B)
    return jnp.concatenate([o_a, o_b], axis=-1) @ w_out

def conv_mixer(h, w_in, conv_w, w_out):
    L = h.shape[1]
    b_gate, c_gate, xin = jnp.split(h @ w_in, 3, axis=-1)
    u = jnp.pad(c_gate * xin, ((0, 0), (CONV_W // 2, CONV_W // 2), (0, 0)))
    y = sum(conv_w[j] * u[:, j:j + L] for j in range(CONV_W))
    return (b_gate * y) @ w_out

def setup_inputs(seed: int = 0) -> dict:
    key = jax.random.key(seed)
    ks = jax.random.split(key, 24)
    D = D_MODEL

    def nrm(k, shape, s):
        return jax.random.normal(k, shape, jnp.float32) * s

    return {
        'x_prompt': nrm(ks[0], (BATCH, SEQ, D), 1.0),
        'x_sample': nrm(ks[1], (DEC_BATCH, DEC_SEQ, D), 1.0),
        'c': nrm(ks[2], (DEC_BATCH, D), 1.0),
        'state_hgrn': nrm(ks[3], (DEC_BATCH, N_EVEN, 2, A_HEADS, A_DK, A_DV), 0.5),
        'cache_k': nrm(ks[4], (DEC_BATCH, N_EVEN, B_HEADS, PAST_LEN, B_DH), 1.0),
        'cache_v': nrm(ks[5], (DEC_BATCH, N_EVEN, B_HEADS, PAST_LEN, B_DH), 1.0),
        'c_ctx': nrm(ks[6], (D,), 1.0),
        'mod_w': nrm(ks[7], (DEPTH, D, N_MOD * D), D ** -0.5),
        'mod_b': nrm(ks[8], (DEPTH, N_MOD * D), 0.02),
        'norm_pre': 1.0 + nrm(ks[9], (DEPTH, 3, D), 0.02),
        'norm_post': 1.0 + nrm(ks[10], (DEPTH, 3, D), 0.02),
        'ffn_w_in': nrm(ks[11], (DEPTH, 2, D, 2 * D_FF), D ** -0.5),
        'ffn_w_out': nrm(ks[12], (DEPTH, 2, D_FF, D), D_FF ** -0.5),
        'ab_w_in': nrm(ks[13], (N_EVEN, D, AB_IN), D ** -0.5),
        'ab_w_out': nrm(ks[14], (N_EVEN, D_A + D_B, D), (D_A + D_B) ** -0.5),
        'a_lb': nrm(ks[15], (N_EVEN, 2, D_A), 1.0),
        'a_gnorm': 1.0 + nrm(ks[16], (N_EVEN, A_DV), 0.02),
        'b_rpb': nrm(ks[17], (N_EVEN, B_HEADS, 2 * NA_ROWS - 1, 2 * NA_COLS - 1), 0.1),
        'cv_w_in': nrm(ks[18], (N_ODD, D, 3 * D), D ** -0.5),
        'cv_conv': nrm(ks[19], (N_ODD, CONV_W, D), CONV_W ** -0.5),
        'cv_w_out': nrm(ks[20], (N_ODD, D, D), D ** -0.5),
    }

def reference(x_prompt, x_sample, c, state_hgrn, cache_k, cache_v, c_ctx, mod_w, mod_b,
              norm_pre, norm_post, ffn_w_in, ffn_w_out, ab_w_in, ab_w_out, a_lb, a_gnorm,
              b_rpb, cv_w_in, cv_conv, cv_w_out):
    lb_all = hgrn2_lower_bounds(a_lb)
    xp, xs = x_prompt, x_sample
    new_s, new_k, new_v = [], [], []
    for l in range(DEPTH):
        mod_p = adaln(c_ctx[None, :], mod_w[l], mod_b[l])
        mod_s = adaln(c, mod_w[l], mod_b[l])
        xp = post_residual(xp, swiglu(pre_norm(xp, mod_p, 0, norm_pre[l, 0]), ffn_w_in[l, 0], ffn_w_out[l, 0]),
                           mod_p, 0, norm_post[l, 0], 0.5)
        xs = post_residual(xs, swiglu(pre_norm(xs, mod_s, 0, norm_pre[l, 0]), ffn_w_in[l, 0], ffn_w_out[l, 0]),
                           mod_s, 0, norm_post[l, 0], 0.5)
        hp = pre_norm(xp, mod_p, 1, norm_pre[l, 1])
        hs = pre_norm(xs, mod_s, 1, norm_pre[l, 1])
        j = l // 2
        if l % 2 == 0:
            op, s_fin, k_ctx, v_ctx = even_mixer_context(hp, ab_w_in[j], ab_w_out[j], lb_all[j], a_gnorm[j])
            new_s.append(s_fin)
            new_k.append(k_ctx)
            new_v.append(v_ctx)
            os_ = even_mixer_latent(hs, ab_w_in[j], ab_w_out[j], lb_all[j], a_gnorm[j], b_rpb[j],
                                    state_hgrn[:, j], cache_k[:, j], cache_v[:, j])
        else:
            op = conv_mixer(hp, cv_w_in[j], cv_conv[j], cv_w_out[j])
            os_ = conv_mixer(hs, cv_w_in[j], cv_conv[j], cv_w_out[j])
        xp = post_residual(xp, op, mod_p, 1, norm_post[l, 1], 1.0)
        xs = post_residual(xs, os_, mod_s, 1, norm_post[l, 1], 1.0)
        xp = post_residual(xp, swiglu(pre_norm(xp, mod_p, 2, norm_pre[l, 2]), ffn_w_in[l, 1], ffn_w_out[l, 1]),
                           mod_p, 2, norm_post[l, 2], 0.5)
        xs = post_residual(xs, swiglu(pre_norm(xs, mod_s, 2, norm_pre[l, 2]), ffn_w_in[l, 1], ffn_w_out[l, 1]),
                           mod_s, 2, norm_post[l, 2], 0.5)
    state_hgrn_new = jnp.stack(new_s, axis=1)
    cache_k_new = jnp.stack(new_k, axis=1)
    cache_v_new = jnp.stack(new_v, axis=1)
    return (xp, xs, state_hgrn_new, cache_k_new, cache_v_new)


_drawn_inputs = setup_inputs


def setup_inputs(seed=0):
    import zlib

    import numpy as np

    out = dict(_drawn_inputs(seed))
    spreads = {}
    factors = {'norm_post': 2.95, 'a_gnorm': 4.979, 'b_rpb': 5.025}
    for name, (base, spread) in spreads.items():
        noise = np.random.default_rng([zlib.crc32(name.encode()), seed]).standard_normal(out[name].shape)
        drawn = base * np.exp(spread * noise) if base else spread * noise
        out[name] = __import__('jax').numpy.asarray(drawn.astype(out[name].dtype))
    for name, factor in factors.items():
        out[name] = (out[name] * factor).astype(out[name].dtype)
    return out
```

```python
from contextlib import ExitStack

import numpy as np

import concourse.bass as bass
from concourse import mybir

P = 128
D_MODEL, SEQ, DEC_SEQ, DEPTH = 1024, 128, 256, 2
NT = SEQ + DEC_SEQ
GROUPS = ((0, SEQ), (SEQ, NT))
KD = D_MODEL // P
D_FF = 2816
KF = D_FF // P
D_A = D_MODEL // 2
HEADS_A, HEADS_B, DH = 4, 8, 64
AB_IN = 8 * D_A
GRID_W, NA_COLS, NA_ROWS, ROWS = 64, 16, 8, DEC_SEQ // 64
RPB_W, RPB_H = 2 * NA_COLS - 1, 2 * NA_ROWS - 1
TOKS = NT // P
UNITS = HEADS_A * TOKS
EPS = 1e-6
LB_MAX = 1.0 - 1e-4
LEVELS = 7
PADDED = NT + 3
RING = 6
NEG = -1e30

F32 = mybir.dt.float32
F32R = mybir.dt.float32r
I32 = mybir.dt.int32
ALU = mybir.AluOpType
ACT = mybir.ActivationFunctionType
AX = mybir.AxisListType

PAR_MOD, PAR_PRE, PAR_POST, PAR_CONV, PAR_LB, PAR_GN, PAR_COND = 0, 144, 192, 240, 264, 272, 273
PAR_ROWS = 289

SUBLAYERS = (("ffn", 0), ("even", 0), ("ffn", 1), ("ffn", 2), ("odd", 0), ("ffn", 3))
HALF = (0.5, 1.0, 0.5, 0.5, 1.0, 0.5)


BUBBLE = ("modB", "modD", "modE", "modF", "modG")
MOD_GROUPS = {"mod0": 2, "modA": 2, "modB": 1, "modC": 9, "modD": 1, "modE": 1, "modF": 1, "modG": 1}


def first_group(st):
    names = list(MOD_GROUPS)
    return sum(MOD_GROUPS[n] for n in names[:names.index(st)])


MOD_BANK = [7 - g % 2 for g in range(18)]
MOD_BANK[5:14] = [2, 3, 2, 7, 2, 7, 2, 7, 2]


def constants():
    s = np.arange(P)[:, None]
    c = np.arange(P // 2)[None, :]
    masks = np.zeros((P, 2 * LEVELS, P // 2), np.int32)
    for lv in range(LEVELS):
        b = 1 << lv
        same = (s // (2 * b)) == (c // b)
        masks[:, 2 * lv] = same & ((s // b) % 2 == 0)
        masks[:, 2 * lv + 1] = same & ((s // b) % 2 == 1)
    q = np.arange(P) % GRID_W
    c0 = np.clip(q - NA_COLS // 2, 0, GRID_W - NA_COLS)[:, None]
    k = np.arange(GRID_W)[None, :]
    window = np.where((k >= c0) & (k < c0 + NA_COLS), 0.0, NEG).astype(np.float32)
    order = np.concatenate([np.arange(64)[::-1], 64 + np.arange(64)[::-1]])
    flip = np.zeros((P, P), np.float32)
    flip[order, np.arange(P)] = DH ** 0.5
    return np.eye(P, dtype=np.float32), masks, window[order], flip


def plan():
    stages, slot, split, mod = {}, 0, 0, 0
    kinds = []

    def add(name, n, kind):
        nonlocal slot, split, mod
        stages[name] = dict(a=slot, m=split, q=mod, n=n)
        slot += n
        for _ in range(n):
            if kind == "split":
                split += 1
            else:
                mod += 1
            kinds.append((kind, split, mod))

    add("mod0", 4 * MOD_GROUPS["mod0"], "mod")
    for s, (kind, _) in enumerate(SUBLAYERS):
        add(f"in{s}", {"ffn": 22, "even": 16, "odd": 12}[kind], "split")
        if s < 2:
            add(("modA", "modC")[s], 4 * MOD_GROUPS[("modA", "modC")[s]], "mod")
        add(f"out{s}", {"ffn": 12, "even": 4, "odd": 4}[kind], "split")
        if s < 5:
            add(BUBBLE[s], 4 * MOD_GROUPS[BUBBLE[s]], "mod")
    return stages, kinds


def trunk(nc, x_prompt, x_sample, c, state_hgrn, cache_k, cache_v, c_ctx, mod_w, mod_b, norm_pre, norm_post,
          ffn_w_in, ffn_w_out, ab_w_in, ab_w_out, a_lb, a_gnorm, b_rpb, cv_w_in, cv_conv, cv_w_out,
          identity, level_masks, window_mask, flip_scaled,
          y_prompt, y_sample, state_new, cache_k_new, cache_v_new, upto=6):
    stages, kinds = plan()
    ctx = ExitStack()
    with ctx:
        def sb(name, shape, dt=F32):
            return ctx.enter_context(nc.sbuf_tensor(name, shape, dt))

        def sem(name):
            return ctx.enter_context(nc.semaphore(name))

        X = sb("X", [P, KD, NT])
        RAW = sb("RAW", [P, RING, 8, 256])
        WH = sb("WH", [P, 4, 8, P], F32R)
        WL = sb("WL", [P, 4, 8, P], F32R)
        TT = sb("TT", [P, 4, NT])
        SQ = sb("SQ", [P, 2, NT])
        ACC = sb("ACC", [P, NT])
        ROOT = sb("ROOT", [P, NT])
        RSTD = sb("RSTD", [P, NT])
        IDENT = sb("IDENT", [P, P])
        ONES = sb("ONES", [P, P])
        LMASK = sb("LMASK", [P, 2 * LEVELS, P // 2], I32)
        WINDOW = sb("WINDOW", [P, GRID_W])
        FLIP = sb("FLIP", [P, P])
        PAR = sb("PAR", [P, NT])
        COND = sb("COND", [P, KD, 32])
        ROWS = sb("ROWS", [P, 256])
        MOD = sb("MOD", [P, 144, 2])
        CA = sb("CA", [P, 6, KD, 2])
        CC = sb("CC", [P, 6, KD, 2])
        LBT = sb("LBT", [P, 4, 8])
        SMALL = sb("SMALL", [P, 3, 4])
        EPSC = sb("EPSC", [P, 1])
        with nc.sbuf_tensor("OUTF", [P, KD, NT], F32) as OUTF:
            pass
        HH = sb("HH", [P, KD, NT], F32R)
        HL = sb("HL", [P, KD, NT], F32R)
        MIX_WORDS = 17152
        with nc.sbuf_tensor("AH", [P, KF, NT], F32R) as AH:
            with nc.sbuf_tensor("AL", [P, KF, NT], F32R) as AL:
                pass
        MIX = sb("MIX", [P, MIX_WORDS])

        def mix(at, *shape):
            n = int(np.prod(shape))
            v = MIX[:, at:at + n]
            if len(shape) == 2:
                return v.rearrange("p (a b) -> p a b", a=shape[0])
            if len(shape) == 3:
                return v.rearrange("p (a b c) -> p a b c", a=shape[0], b=shape[1])
            return v

        W15 = 4 * NT
        BQ, BK, BV = mix(0, 4, NT), mix(W15, 4, NT), mix(2 * W15, TOKS, 512)
        BIAS = mix(3 * W15, 6, GRID_W)
        CKT, CV = mix(3 * W15 + 384, 4, P), mix(3 * W15 + 896, HEADS_B, DH)
        AT0 = 3 * W15 + 1408
        QF, KFW, FF, FB, KBW, V, G = (mix(AT0 + i * W15, 4, NT) for i in range(7))
        VT = mix(AT0 + 5 * W15, TOKS, 512)
        CKR = TT[:, :, :].rearrange("p a b -> p (a b)")[:, 0:512]
        QB = BK
        ATT = mix(2 * W15, UNITS, P)
        ST = mix(3 * W15 + 384, 8, P)
        OUTM = mix(AT0 + 2 * W15, KD, NT)
        KS = TT[:, :, :].rearrange("p a b -> p (a b)").rearrange("p (u t) -> p u t", u=UNITS)
        KTOK = TT[:, :, :].rearrange("p a b -> p (a b)")[:, 0:1024].rearrange("p (h j t) -> p h j t", h=2, j=4)
        KOUT = SQ[:, :, :].rearrange("p a b -> p (a b)")[:, 0:512]
        CB, CG = mix(0, KD, PADDED), mix(KD * PADDED, KD, PADDED)
        U = mix(2 * KD * PADDED, 2, PADDED)
        Y = mix((2 * KD + 2) * PADDED, PADDED)
        OUTC = mix((2 * KD + 3) * PADDED + 1, KD, NT)
        XS = mix(0, TOKS, D_MODEL)
        PS = TT[:, 0:1, :].rearrange("p a (t n) -> p (a t) n", t=3)

        bank = [ctx.enter_context(nc.psum_tensor(f"bank{i}", [P, 512], F32)) for i in range(8)]

        raw_landed = [sem(f"raw_landed{i}") for i in range(RING)]
        setup_landed = sem("setup_landed")
        x_landed = sem("x_landed")
        half_hi = sem("half_hi")
        half_ready = sem("half_ready")
        half_used = sem("half_used")
        mod_used = sem("mod_used")
        mod_rows = sem("mod_rows")
        mod_turned = sem("mod_turned")
        mod_cols = sem("mod_cols")
        coef_ready = sem("coef_ready")
        coef_step = sem("coef_step")
        tp_done = sem("tp_done")
        par_ready = sem("par_ready")
        cond_ready = sem("cond_ready")
        lb_step = sem("lb_step")
        const_set = sem("const_set")
        x_ready = sem("x_ready")
        xsq_done = sem("xsq_done")
        stat_done = sem("stat_done")
        root_done = sem("root_done")
        rstd_done = sem("rstd_done")
        h_scaled = sem("h_scaled")
        h_full = sem("h_full")
        h_hi = sem("h_hi")
        h_ready = sem("h_ready")
        silu_done = sem("silu_done")
        gated = sem("gated")
        act_hi = sem("act_hi")
        act_ready = sem("act_ready")
        out_sq = sem("out_sq")
        out_done = sem("out_done")
        sq_added = sem("sq_added")
        delta = sem("delta")
        proj_out = sem("proj_out")
        ctx_landed, ctx_turned, ctx_ready = sem("ctx_landed"), sem("ctx_turned"), sem("ctx_ready")
        bias_landed, bias_ready = sem("bias_landed"), sem("bias_ready")
        s_mm, s_max, s_exp = sem("s_mm"), sem("s_max"), sem("s_exp")
        p_inv, p_ready, p_turned, p_copied = sem("p_inv"), sem("p_ready"), sem("p_turned"), sem("p_copied")
        pv_done, ob_done = sem("pv_done"), sem("ob_done")
        kout_turned, kout_ready, kv_stored = sem("kout_turned"), sem("kout_ready"), sem("kv_stored")
        cat_hi, cat_ready = sem("cat_hi"), sem("cat_ready")
        sig_done, prep = sem("sig_done"), sem("prep")
        diag_mm, diag_out = sem("diag_mm"), sem("diag_out")
        lvl_mm, lvl_out, lvl_q, lvl_k, lvl_t = (sem(n) for n in ("lvl_mm", "lvl_out", "lvl_q", "lvl_k", "lvl_t"))
        state_landed, state_stored = sem("state_landed"), sem("state_stored")
        k_turned, k_copied, st_mm, st_ready = sem("k_turned"), sem("k_copied"), sem("st_mm"), sem("st_ready")
        o_mm, o_sq, o_copied, o_stat, o_root = (sem(n) for n in ("o_mm", "o_sq", "o_copied", "o_stat", "o_root"))
        o_step = sem("o_step")
        pads_set, conv_step, conv_done = sem("pads_set"), sem("conv_step"), sem("conv_done")
        y_copied, y_stored = sem("y_copied"), sem("y_stored")

        def ring_at(st, j):
            return (stages[st]["a"] + j) % RING, (stages[st]["a"] + j) // RING

        def src_of(st, n):
            def cols(w, col, k0=0, k1=8):
                return w.rearrange("(k p) n -> p k n", p=P)[:, k0:k1, bass.ds(col, 256)]
            if st.startswith("mod"):
                t = 8 * first_group(st) + 2 * n
                return cols(mod_w[t // 72], (t % 72) * P), 8
            s = int(st[-1])
            kind, f = SUBLAYERS[s]
            if kind == "ffn":
                if st.startswith("in"):
                    return cols(ffn_w_in[f // 2, f % 2], (n // 2) * 256 + (n % 2) * D_FF), 8
                q, r = divmod(n, 3)
                return cols(ffn_w_out[f // 2, f % 2], q * 256, 8 * r, min(8 * r + 8, KF)), min(8, KF - 8 * r)
            if kind == "even":
                if st.startswith("in"):
                    return cols(ab_w_in[0], AB_ORDER[n] * 256), 8
                return cols(ab_w_out[0], n * 256), 8
            return cols((cv_w_in if st.startswith("in") else cv_w_out)[0], n * 256), 8

        AB_ORDER = [10, 11, 12, 13, 14, 15, 0, 1, 6, 7, 2, 3, 4, 5, 8, 9]

        def used(st, n, b):
            return 4 + 2 * (stages[st]["m"] + n) + b + 1

        def split_act(e, st, jj, nk, i=0):
            yield_b = []
            p, uses = ring_at(st, jj)
            m = stages[st]["m"] + jj
            for b in range(2):
                def half(b=b):
                    if b == 0:
                        e.wait_ge(raw_landed[p], (i + uses + 1) * 16)
                    e.wait_ge(half_used, i * 12 + (2 * m + b + 1))
                    e.activation(WH[:, (2 * m + b) % 4, 0:nk, :], RAW[:, p, 0:nk, b * P:(b + 1) * P],
                                 ACT.Copy).then_inc(half_hi, 1)
                yield_b.append(half)
            return yield_b

        def split_dve(e, st, jj, nk, i=0):
            out = []
            p, _ = ring_at(st, jj)
            m = stages[st]["m"] + jj
            for b in range(2):
                def half(b=b):
                    k = (2 * m + b) % 4
                    e.wait_ge(half_hi, i * 12 + (2 * m + b + 1))
                    e.tensor_tensor(WL[:, k, 0:nk, :], RAW[:, p, 0:nk, b * P:(b + 1) * P],
                                    WH[:, k, 0:nk, :].bitcast(F32), ALU.subtract).then_inc(half_ready, 1)
                out.append(half)
            return out

        def out_nk(st, n):
            kind = SUBLAYERS[int(st[-1])][0]
            return min(8, KF - 8 * (n % 3)) if kind == "ffn" and st.startswith("out") else 8

        def ahead(e, split, s, part, n):
            st, n2 = f"{part}{s}", n + 2
            if n2 >= stages[st]["n"]:
                if part == "out" or SUBLAYERS[s][0] == "even":
                    return [lambda: None] * 2
                st, n2 = f"out{s}", n2 - stages[st]["n"]
            return split(e, st, n2, out_nk(st, n2))

        def ffn_pairs(e, body):
            body(0, 0)
            with e.Fori(0, 3) as i:
                for j in (2, 4, 6):
                    body(i, j)
            body(0, 20)

        def pe_half(e, st, jj, xh, xl, nk, out, first, last, i=0, h_wait=None):
            H = 2 * stages[st]["m"] + jj
            e.wait_ge(half_ready, i * 12 + (H + 1))
            k = H % 4
            for kk in range(nk):
                if h_wait is not None:
                    e.wait_ge(h_ready, h_wait + kk + 1)
                e.matmul(out, WH[:, k, kk, :], xh(kk), start=(first and kk == 0), stop=False)
                e.matmul(out, WH[:, k, kk, :], xl(kk), start=False, stop=False)
                mm = e.matmul(out, WL[:, k, kk, :], xh(kk), start=False, stop=(last and kk == nk - 1))
            mm.then_inc(half_used, 1)

        def cols3(t):
            return t[:, 0:NT]

        hh = lambda kk: HH[:, kk, :]
        hl = lambda kk: HL[:, kk, :]

        def halves(t, b):
            return t.rearrange("p h n -> p (h n)").rearrange("p (m w i) -> p m w i", w=2, i=b)

        def total(t, b, side):
            v = halves(t, b)[:, :, side, 0:1]
            return v.broadcast_to([P, UNITS * P // (2 * b), b])

        PREP = 23
        OB = [0, 1, 2, 5]

        block = ctx.enter_context(nc.Block())

        @block.sync
        def _(sp):
            xr = [x_prompt[0], x_sample[0, 0:P], x_sample[0, P:2 * P]]
            for t in range(TOKS):
                sp.dma_start(XS[:, t, :], xr[t]).then_inc(x_landed, 16)
            sp.dma_start(IDENT[:], identity).then_inc(setup_landed, 16)
            rows = [(PAR_MOD, mod_b.rearrange("l (t p) -> (l t) p", p=P)),
                    (PAR_PRE, norm_pre.rearrange("l j (t p) -> (l j t) p", p=P)),
                    (PAR_POST, norm_post.rearrange("l j (t p) -> (l j t) p", p=P)),
                    (PAR_CONV, cv_conv.rearrange("o w (t p) -> (o w t) p", p=P)),
                    (PAR_LB, a_lb.rearrange("o w (t p) -> (o w t) p", p=P)),
                    (PAR_GN, a_gnorm),
                    (PAR_COND, c_ctx.rearrange("(t p) -> t p", p=P)),
                    (PAR_COND + 8, c[0].rearrange("(t p) -> t p", p=P))]
            n_par = 0
            for r0, src in rows:
                done, n = 0, src.shape[0]
                while done < n:
                    tile, at = divmod(r0 + done, P)
                    k = min(n - done, P - at)
                    sp.dma_start(PS[at:at + k, tile, :], src[done:done + k, :]).then_inc(setup_landed, 16)
                    done += k
                    n_par += 1
            assert n_par == 10, n_par
            sp.dma_start(LMASK[:], level_masks).then_inc(setup_landed, 16)
            sp.dma_start(WINDOW[:], window_mask).then_inc(setup_landed, 16)
            sp.dma_start(FLIP[:], flip_scaled).then_inc(setup_landed, 16)

            def load(st, jj, src, nk, i=0):
                p, _ = ring_at(st, jj)
                return sp.dma_start(RAW[:, p, 0:nk, :], src).then_inc(raw_landed[p], 16)

            def wait_ring(g):
                if g >= RING:
                    kind, m, q = kinds[g - RING]
                    if kind == "split":
                        sp.wait_ge(half_ready, 2 * m)
                    else:
                        sp.wait_ge(mod_used, q)

            for st, d in stages.items():
                if not st.startswith("mod") and int(st[-1]) >= upto or st == BUBBLE[min(upto, 5) - 1] and upto < 6:
                    break
                if st.startswith("in") and SUBLAYERS[int(st[-1])][0] == "ffn":
                    for n in range(RING):
                        wait_ring(d["a"] + n)
                        load(st, n, *src_of(st, n))
                    w = ffn_w_in[SUBLAYERS[int(st[-1])][1] // 2, SUBLAYERS[int(st[-1])][1] % 2]
                    w = w.rearrange("(k p) n -> p k n", p=P)
                    with sp.Fori(0, 2) as i:
                        for j in range(RING):
                            sp.wait_ge(half_ready, i * 12 + 2 * (d["m"] + j + 1))
                            col = i * 768 + (768 + (j // 2) * 256 + (j % 2) * D_FF)
                            load(st, j, w[:, :, bass.ds(col, 256)], 8)
                    for n in range(18, 22):
                        wait_ring(d["a"] + n)
                        load(st, n, *src_of(st, n))
                else:
                    for n in range(d["n"]):
                        wait_ring(d["a"] + n)
                        load(st, n, *src_of(st, n))

        @block.gpsimd
        def _(pool):
            pool.memset(ONES[:], 1.0)
            pool.memset(COND[:], 0.0)
            pool.memset(EPSC[:], EPS).then_inc(const_set, 1)
            if upto < 2:
                return
            pool.wait_ge(setup_landed, 16 * 14)
            pool.wait_ge(h_ready, 16)
            pool.dma_start(CKR, cache_k[0, 0].rearrange("h t d -> t h d")).then_inc(ctx_landed, 16)
            pool.dma_start(CV, cache_v[0, 0].rearrange("h t d -> t h d")).then_inc(ctx_landed, 16)
            for h in range(HEADS_B):
                if h >= 1:
                    pool.wait_ge(s_mm, 3 * h)
                for j in range(2):
                    off = h * RPB_H * RPB_W + (5 - j) * RPB_W + NA_COLS - 1 - (GRID_W - 1)
                    pool.dma_start(BIAS[64 * j:64 * j + 64], bass.AP(
                        tensor=b_rpb.tensor, offset=b_rpb.offset + off,
                        ap=[[1, GRID_W], [RPB_W, 6], [1, GRID_W]])).then_inc(bias_landed, 16)
                pool.wait_ge(bias_landed, 32 * (h + 1))
                pool.tensor_tensor(BIAS, BIAS, WINDOW[:].rearrange("p (a b) -> p a b", a=1)
                                   .broadcast_to([P, 6, GRID_W]), ALU.add).then_inc(bias_ready, 1)
            pool.wait_ge(pv_done, 24)
            pool.dma_start(ST, state_hgrn[0, 0].rearrange("w h k v -> k (w h) v")).then_inc(state_landed, 16)
            for lv in range(LEVELS):
                b = 1 << lv
                for w in range(2):
                    pool.wait_ge(lvl_mm, 2 * lv + w + 1)
                    if lv == 0:
                        pool.wait_ge(prep, PREP)
                    else:
                        pool.wait_ge(lvl_t, 2 * (lv - 1) + w + 1)
                    k = halves((KFW, KBW)[w], b)[:, :, w, :]
                    pool.tensor_tensor(k, k, total((FF, FB)[w], b, 1 - w), ALU.mult).then_inc(lvl_k, 1)

        @block.scalar
        def _(act):
            act.wait_ge(par_ready, 1)
            act.wait_ge(const_set, 1)
            act.activation(COND[:, :, 0:2], PAR[:, PAR_COND:PAR_COND + 16].rearrange("p (g k) -> p k g", g=2),
                           ACT.Silu).then_inc(cond_ready, 1)
            act.wait_ge(lb_step, 1)
            act.activation(LBT[:, 0, :], LBT[:, 1, :], ACT.Exp).then_inc(lb_step, 1)

            def mod_rows_out(g):
                B = bank[MOD_BANK[g]]
                act.wait_ge(mod_used, 4 * g + 4)
                if g >= 1:
                    act.wait_ge(mod_turned, g)
                act.activation(ROWS[:], B[:, 0:256], ACT.Copy).then_inc(mod_rows, 1)

            def mod_cols_out(g):
                B = bank[MOD_BANK[g]]
                act.wait_ge(mod_turned, g + 1)
                act.activation(MOD[:, 8 * g:8 * g + 8, :].rearrange("p (q h) g -> p h q g", h=2),
                               B[:, 0:16].rearrange("p (h q g) -> p h q g", h=2, q=4),
                               ACT.Copy).then_inc(mod_cols, 1)

            def root(src, n_in, when):
                act.wait_ge(*when)
                act.activation(ROOT[:], cols3(src), ACT.Sqrt, bias=EPSC[:, 0:1],
                               scale=1.0 / n_in).then_inc(root_done, 1)

            def pre(s):
                for pp in range(4):
                    act.wait_ge(x_ready, 4 * s + pp + 1)
                    if pp >= 2:
                        act.wait_ge(stat_done, 5 * s + pp - 1)
                    act.activation(SQ[:] if pp % 2 == 0 else TT[:, 2:4, :], X[:, 2 * pp:2 * pp + 2, :],
                                   ACT.Square).then_inc(xsq_done, 1)
                if s:
                    mod_rows_out(first_group(BUBBLE[s - 1]))
                root(bank[1], D_MODEL, (stat_done, 5 * s + 4))
                if s:
                    mod_cols_out(first_group(BUBBLE[s - 1]))
                act.wait_ge(coef_ready, 3 * s + 2)
                for d in range(KD):
                    act.wait_ge(h_scaled, 8 * s + d + 1)
                    for g, (t0, t1) in enumerate(GROUPS):
                        a = act.activation(HH[:, d, t0:t1], TT[:, d % 2, t0:t1], ACT.Identity,
                                           bias=MOD[:, 24 * s + d, g:g + 1], scale=CA[:, s, d, g:g + 1])
                    a.then_inc(h_hi, 1)
                for n in range(2):
                    for half in split_act(act, f"in{s}", n, 8):
                        half()

            def out_tile(s, OUT, st, n, b, d):
                act.wait_ge(half_used, used(st, n, b))
                if d >= 2:
                    act.wait_ge(sq_added, 8 * s + d - 1)
                act.activation(SQ[:, d % 2, :], cols3(bank[4 + d % 4]), ACT.Square).then_inc(out_sq, 1)
                if d == 0:
                    act.wait_ge(coef_ready, 3 * s + 3)
                for g, (t0, t1) in enumerate(GROUPS):
                    a = act.activation(OUT[:, d, t0:t1], bank[4 + d % 4][:, t0:t1], ACT.Copy,
                                       scale=CC[:, s, d, g:g + 1])
                a.then_inc(out_done, 1)

            def post(s):
                root(bank[0], D_MODEL, (stat_done, 5 * s + 5))

            def ffn(s):
                f, st = SUBLAYERS[s][1], f"in{s}"

                def pair(i, j):
                    nxt = [split_act(act, st, j + 2 + q, 8, i) for q in range(2)] if j < 20 else \
                        [split_act(act, f"out{s}", q, 8) for q in range(2)]
                    base = 22 * f + j
                    for b in range(2):
                        nxt[0][b]()
                        act.wait_ge(half_used, i * 12 + used(st, j, b))
                        act.wait_ge(gated, i * 6 + (base + b + 1))
                        act.activation(TT[:, b, :], cols3(bank[b]), ACT.Silu).then_inc(silu_done, 1)
                    nxt[1][0]()
                    nxt[1][1]()
                    for b in range(2):
                        act.wait_ge(gated, i * 6 + (2 + base + b + 1))
                        act.activation(AH[:, bass.ds(i * 6 + (j + b), 1), :], TT[:, 2 + b:3 + b, :],
                                       ACT.Copy).then_inc(act_hi, 1)

                ffn_pairs(act, pair)
                if s == 0:
                    mod_rows_out(2)
                    mod_cols_out(2)
                    mod_rows_out(3)
                    mod_cols_out(3)
                for n in range(12):
                    for half in ahead(act, split_act, s, "out", n):
                        half()
                    if n % 3 == 2:
                        for b in range(2):
                            out_tile(s, OUTF, f"out{s}", n, b, 2 * (n // 3) + b)

            def even(s):
                def proj(tau):
                    ahead(act, split_act, s, "in", tau // 2)[tau % 2]()
                    part, q = divmod(AB_ORDER[tau // 2] * 2 + tau % 2, 4)
                    if part in (3, 7):
                        dst = (VT if part == 3 else BV)[:, :, (q // 2) * 256:(q // 2) * 256 + 256]
                        act.wait_ge(half_used, used(f"in{s}", tau // 2, 1))
                        B = bank[tau % 4]
                        if tau % 2 == 0:
                            a = act.activation(dst[:, 0:2, :], B[:].rearrange("p (t n) -> p t n", t=2), ACT.Copy)
                        else:
                            a = act.activation(dst[:, 2, :], B[:, 0:256], ACT.Copy)
                        a.then_inc(proj_out, 1)
                        return
                    dst = {0: QF, 1: FF, 2: FB, 4: G, 5: BQ, 6: BK}[part][:, q, :]
                    act.wait_ge(half_used, used(f"in{s}", tau // 2, tau % 2))
                    act.activation(dst, cols3(bank[tau % 4]), ACT.Copy).then_inc(proj_out, 1)

                for tau in range(12):
                    proj(tau)
                act.wait_ge(ctx_turned, 1)
                act.activation(CKT.rearrange("p a b -> p (a b)"), bank[6][:], ACT.Copy).then_inc(ctx_ready, 1)
                act.wait_ge(proj_out, 12)
                act.dma_start(cache_v_new[0, 0].rearrange("h t d -> t h d"),
                              BV[:, 0, :].rearrange("p (h d) -> p h d", h=HEADS_B)).then_inc(kv_stored, 16)
                for step in range(24 + 3):
                    u = step
                    if u < 24:
                        act.wait_ge(s_max, 2 * u + 2)
                        if u >= 4:
                            act.wait_ge(p_turned, u - 3)
                        n = P if u % 3 == 0 else NT
                        act.activation(TT[:, u % 4, 0:n], bank[4 + u % 2][:, 0:n], ACT.Exp,
                                       bias=SMALL[:, 0, u % 4:u % 4 + 1], scale=DH ** -0.5,
                                       accum_out=SMALL[:, 1, u % 4:u % 4 + 1]).then_inc(s_exp, 1)
                    u = step - 2
                    if 0 <= u < 24:
                        n = P if u % 3 == 0 else NT
                        act.wait_ge(p_turned, u + 1)
                        if u >= 2:
                            act.wait_ge(pv_done, u - 1)
                        act.activation(SQ[:, u % 2, 0:n], bank[6][:, 0:n], ACT.Copy).then_inc(p_copied, 1)
                    u = step - 3
                    if 0 <= u < 24 and u % 6 == 5:
                        act.wait_ge(pv_done, u + 1)
                        act.activation(BQ[:, u // 6, :], cols3(bank[7]), ACT.Copy).then_inc(ob_done, 1)
                    if step < 20:
                        proj(12 + step)
                g0 = first_group("modC")
                mod_rows_out(g0)
                mod_cols_out(g0)
                act.wait_ge(kout_turned, 1)
                act.activation(KOUT, bank[6][:], ACT.Copy).then_inc(kout_ready, 1)
                act.wait_ge(kout_ready, 1)
                act.dma_start(cache_k_new[0, 0].rearrange("h t d -> t h d"),
                              KOUT.rearrange("p (h d) -> p h d", h=HEADS_B)).then_inc(kv_stored, 16)
                act.wait_ge(proj_out, 32)
                for w, (z, k) in enumerate(((FF, KFW), (FB, KBW))):
                    act.activation(k, z, ACT.Sigmoid, scale=-1.0).then_inc(sig_done, 1)
                    act.wait_ge(sig_done, 2 * w + 1)
                    act.activation(z, z, ACT.Sigmoid).then_inc(sig_done, 1)
                act.activation(TT[:], G, ACT.Sigmoid).then_inc(sig_done, 1)
                mod_rows_out(g0 + 1)
                mod_cols_out(g0 + 1)
                for ht in range(4):
                    act.activation(HH[:, 4 + ht, :], BQ[:, ht, :], ACT.Copy).then_inc(cat_hi, 1)
                mod_rows_out(g0 + 2)
                mod_cols_out(g0 + 2)
                for g in range(g0 + 3, g0 + 9):
                    mod_rows_out(g)
                    mod_cols_out(g)
                act.wait_ge(kv_stored, 32)
                for h in range(HEADS_A):
                    act.wait_ge(k_turned, h + 1)
                    if h >= 2:
                        act.wait_ge(st_mm, h - 1)
                    act.activation(KTOK[:, h % 2].rearrange("p j t -> p (j t)"), bank[5][:],
                                   ACT.Copy).then_inc(k_copied, 1)
                for h in range(HEADS_A):
                    act.wait_ge(st_ready, 4 * h + 4)
                    if h == 0:
                        act.wait_ge(st_ready, 4 * HEADS_A)
                        for w in range(2):
                            act.dma_start(state_new[0, 0, w].rearrange("h k v -> k h v"),
                                          (KFW, KBW)[w][:, :, 0:P]).then_inc(state_stored, 16)
                    act.wait_ge(o_mm, h + 1)
                    if h >= 2:
                        act.wait_ge(o_stat, h - 1)
                    act.activation(SQ[:, h % 2, :], cols3(bank[OB[h]]), ACT.Square).then_inc(o_sq, 1)
                    act.activation(FF[:, h, :], cols3(bank[OB[h]]), ACT.Copy).then_inc(o_copied, 1)
                    act.wait_ge(o_stat, h + 1)
                    if h >= 1:
                        act.wait_ge(o_step, 4 * (h - 1) + 1)
                    act.activation(ROOT[:], cols3(bank[(6, 3)[h % 2]]), ACT.Sqrt, bias=EPSC[:, 0:1],
                                   scale=1.0 / P).then_inc(o_root, 1)
                    act.wait_ge(o_step, 4 * h + 3)
                    act.activation(HH[:, h, :], FF[:, h, :], ACT.Copy).then_inc(cat_hi, 1)
                act.wait_ge(state_stored, 32)
                for n in range(-2, 4):
                    for half in ahead(act, split_act, s, "out", n):
                        half()
                    for b in range(2 if n >= 0 else 0):
                        out_tile(s, OUTM, f"out{s}", n, b, 2 * n + b)

            def odd(s):
                for tau in range(24):
                    if tau % 2 == 0:
                        for half in ahead(act, split_act, s, "in", tau // 2):
                            half()
                    d = tau % 8
                    if tau < 16:
                        act.wait_ge(half_used, used(f"in{s}", tau // 2, tau % 2))
                        dst = (CB if tau < 8 else CG)[:, d, :]
                        for g, (t0, t1) in enumerate(GROUPS):
                            a = act.activation(dst[:, t0 + 1 + g:t1 + 1 + g], bank[tau % 4][:, t0:t1], ACT.Copy)
                        a.then_inc(proj_out, 1)
                for d in range(KD):
                    act.wait_ge(conv_done, d + 1)
                    if d == 0:
                        act.wait_ge(half_used, used(f"in{s}", 11, 1))
                    for g, (t0, t1) in enumerate(GROUPS):
                        a = act.activation(HH[:, d, t0:t1], CG[:, d, t0 + 1 + g:t1 + 1 + g], ACT.Copy)
                    a.then_inc(cat_hi, 1)
                for n in range(4):
                    for half in ahead(act, split_act, s, "out", n):
                        half()
                    for b in range(2):
                        out_tile(s, OUTC, f"out{s}", n, b, 2 * n + b)

            mod_rows_out(0)
            mod_cols_out(0)
            mod_rows_out(1)
            mod_cols_out(1)
            pre(0)
            for s in range(upto):
                {"ffn": ffn, "even": even, "odd": odd}[SUBLAYERS[s][0]](s)
                post(s)
                if s < upto - 1:
                    pre(s + 1)
            for t in range(TOKS):
                act.wait_ge(y_copied, 2 * t + 2)
                act.dma_start([y_prompt[0], y_sample[0, 0:P], y_sample[0, P:2 * P]][t], XS[:, t, :]) \
                    .then_inc(y_stored, 16)
            act.wait_ge(y_stored, 16 * TOKS)

        @block.vector
        def _(dve):
            dve.sem_inc(gated, 2)
            dve.sem_inc(act_ready, 2)
            dve.wait_ge(tp_done, 1)
            dve.tensor_copy(PAR[:, 0:PAR_ROWS], bank[0][:, 0:PAR_ROWS]).then_inc(par_ready, 1)
            lb_in = PAR[:, PAR_LB:PAR_LB + 8]
            dve.wait_ge(par_ready, 1)
            dve.tensor_tensor(LBT[:, 1, :], lb_in, lb_in, ALU.subtract).then_inc(lb_step, 1)
            dve.wait_ge(lb_step, 2)
            dve.reciprocal(LBT[:, 1, :], LBT[:, 0, :]).then_inc(lb_step, 1)
            dve.wait_ge(lb_step, 3)
            dve.tensor_tensor(LBT[:, 2, :], LBT[:, 0, :], LBT[:, 1, :], ALU.mult).then_inc(lb_step, 1)
            dve.wait_ge(lb_step, 4)
            dve.tensor_tensor(LBT[:, 3, :], LBT[:, 2, :], LBT[:, 2, :], ALU.subtract).then_inc(lb_step, 1)
            dve.wait_ge(lb_step, 5)
            dve.tensor_scalar(LBT[:, 2, :], LBT[:, 3, :], 0.0, LB_MAX, ALU.max, ALU.min).then_inc(lb_step, 1)
            dve.wait_ge(lb_step, 6)
            dve.tensor_scalar(LBT[:, 3, :], LBT[:, 2, :], -1.0, 1.0, ALU.mult, ALU.add).then_inc(lb_step, 1)
            for d in range(KD):
                dve.wait_ge(tp_done, 2 + d)
                x = dve.tensor_copy(X[:, d, :], cols3(bank[1 + d % 4]))
                if d % 2:
                    x.then_inc(x_ready, 1)
                else:
                    x.then_inc(delta, 1)

            def coefficients(g):
                m = MOD[:, 8 * g:8 * g + 8, :]
                dve.wait_ge(mod_cols, g + 1)
                dve.tensor_tensor(m, m, PAR[:, 8 * g:8 * g + 8].rearrange("p (t g) -> p t g", g=1)
                                  .broadcast_to([P, 8, 2]), ALU.add).then_inc(coef_step, 1)
                dve.wait_ge(coef_step, g + 1)
                b, part = divmod(g, 3)
                if part == 0:
                    dve.sem_inc(coef_ready, 1)
                    return
                norm = (PAR_PRE if part == 1 else PAR_POST) + 8 * b
                gain = PAR[:, norm:norm + 8].rearrange("p (t g) -> p t g", g=1).broadcast_to([P, 8, 2])
                if part == 1:
                    c_ = dve.scalar_tensor_tensor(CA[:, b], m, 1.0, gain, ALU.add, ALU.mult)
                else:
                    c_ = dve.scalar_tensor_tensor(CC[:, b], m, HALF[b], gain, ALU.mult, ALU.mult)
                c_.then_inc(coef_ready, 1)

            def rstd(n):
                dve.wait_ge(root_done, n)
                dve.reciprocal(RSTD[:], ROOT[:]).then_inc(rstd_done, 1)
                dve.wait_ge(rstd_done, n)

            def pre(s):
                rstd(2 * s + 1)
                if s:
                    coefficients(first_group(BUBBLE[s - 1]))
                dve.wait_ge(coef_ready, 3 * s + 2)

                def scaled(d):
                    if d >= 2:
                        dve.wait_ge(h_hi, 8 * s + d - 1)
                        dve.wait_ge(h_full, 8 * s + d - 1)
                    dve.tensor_tensor(TT[:, d % 2, :], X[:, d, :], RSTD[:], ALU.mult).then_inc(h_scaled, 1)

                scaled(0)
                for d in range(KD):
                    if d + 1 < KD:
                        scaled(d + 1)
                    dve.wait_ge(h_scaled, 8 * s + d + 1)
                    if d >= 2:
                        dve.wait_ge(h_ready, 8 * s + d - 1)
                    for g, (t0, t1) in enumerate(GROUPS):
                        x = dve.tensor_scalar(TT[:, 2 + d % 2, t0:t1], TT[:, d % 2, t0:t1], CA[:, s, d, g:g + 1],
                                              MOD[:, 24 * s + d, g:g + 1], ALU.mult, ALU.add)
                    x.then_inc(h_full, 1)
                    dve.wait_ge(h_full, 8 * s + d + 1)
                    dve.wait_ge(h_hi, 8 * s + d + 1)
                    dve.tensor_tensor(HL[:, d, :], TT[:, 2 + d % 2, :], HH[:, d, :].bitcast(F32),
                                      ALU.subtract).then_inc(h_ready, 1)
                for n in range(2):
                    for half in split_dve(dve, f"in{s}", n, 8):
                        half()

            def add_square(s, d):
                dve.wait_ge(out_sq, 8 * s + d + 1)
                if d == 0:
                    dve.tensor_copy(ACC[:], SQ[:, 0, :]).then_inc(sq_added, 1)
                else:
                    dve.wait_ge(sq_added, 8 * s + d)
                    dve.tensor_tensor(ACC[:], ACC[:], SQ[:, d % 2, :], ALU.add).then_inc(sq_added, 1)

            def post(s, OUT):
                rstd(2 * s + 2)
                dve.wait_ge(out_done, 4 + 8 * (s + 1))
                for pp in range(4):
                    if pp:
                        dve.wait_ge(x_ready, 4 * s + 4 + pp)
                    dve.tensor_tensor(TT[:, 0:2, :], OUT[:, 2 * pp:2 * pp + 2, :],
                                      RSTD[:].rearrange("p (a n) -> p a n", a=1).broadcast_to([P, 2, NT]),
                                      ALU.mult).then_inc(delta, 1)
                    dve.wait_ge(delta, 4 + 4 * s + pp + 1)
                    dve.tensor_tensor(X[:, 2 * pp:2 * pp + 2, :], X[:, 2 * pp:2 * pp + 2, :], TT[:, 0:2, :],
                                      ALU.add).then_inc(x_ready, 1)

            def ffn(s):
                f, st = SUBLAYERS[s][1], f"in{s}"

                def pair(i, j):
                    nxt = [split_dve(dve, st, j + 2 + q, 8, i) for q in range(2)] if j < 20 else \
                        [split_dve(dve, f"out{s}", q, 8) for q in range(2)]
                    base = 22 * f + j
                    nxt[0][0]()
                    nxt[0][1]()
                    for b in range(2):
                        nxt[1][b]()
                        dve.wait_ge(silu_done, i * 6 + (2 + base + b + 1))
                        dve.wait_ge(half_used, i * 12 + used(st, j + 1, b))
                        dve.wait_ge(act_ready, i * 6 + (base + b + 1))
                        dve.tensor_tensor(TT[:, 2 + b, :], TT[:, b, :], cols3(bank[2 + b]),
                                          ALU.mult).then_inc(gated, 1)
                    for b in range(2):
                        dve.wait_ge(act_hi, i * 6 + (base + b + 1))
                        at = bass.ds(i * 6 + (j + b), 1)
                        dve.tensor_tensor(AL[:, at, :], TT[:, 2 + b:3 + b, :], AH[:, at, :].bitcast(F32),
                                          ALU.subtract).then_inc(act_ready, 1)

                ffn_pairs(dve, pair)
                if s == 0:
                    coefficients(2)
                    coefficients(3)
                for n in range(12):
                    for half in ahead(dve, split_dve, s, "out", n):
                        half()
                    if n % 3 == 2:
                        for b in range(2):
                            add_square(s, 2 * (n // 3) + b)

            def even(s):
                def proj(tau):
                    ahead(dve, split_dve, s, "in", tau // 2)[tau % 2]()

                for tau in range(12):
                    proj(tau)
                for step in range(24 + 3):
                    u = step
                    if u < 24:
                        top = SMALL[:, 0, u % 4:u % 4 + 1]
                        dve.wait_ge(s_mm, u + 1)
                        dve.tensor_reduce(top, bank[4 + u % 2][:, 0:P if u % 3 == 0 else NT], AX.X,
                                          ALU.max, negate=True).then_inc(s_max, 1)
                        dve.wait_ge(s_max, 2 * u + 1)
                        dve.tensor_scalar(top, top, DH ** -0.5, None, ALU.mult).then_inc(s_max, 1)
                    u = step - 1
                    if 0 <= u < 24:
                        n = P if u % 3 == 0 else NT
                        dve.wait_ge(s_exp, u + 1)
                        dve.reciprocal(SMALL[:, 2, u % 4:u % 4 + 1], SMALL[:, 1, u % 4:u % 4 + 1]).then_inc(p_inv, 1)
                        dve.wait_ge(p_inv, u + 1)
                        dve.tensor_scalar(TT[:, u % 4, 0:n], TT[:, u % 4, 0:n], SMALL[:, 2, u % 4:u % 4 + 1], None,
                                          ALU.mult).then_inc(p_ready, 1)
                    if step < 20:
                        proj(12 + step)
                n = [0]

                def tick(x):
                    x.then_inc(prep, 1)
                    n[0] += 1

                dve.wait_ge(sig_done, 4)
                for w, (f, k) in enumerate(((FF, KFW), (FB, KBW))):
                    for h in range(HEADS_A):
                        lb, one_less = LBT[:, 2, 4 * w + h:4 * w + h + 1], LBT[:, 3, 4 * w + h:4 * w + h + 1]
                        tick(dve.tensor_scalar(f[:, h, :], f[:, h, :], one_less, lb, ALU.mult, ALU.add))
                        tick(dve.tensor_scalar(k[:, h, :], k[:, h, :], one_less, None, ALU.mult))
                dve.wait_ge(prep, 16)
                tick(dve.tensor_scalar(FF, FF, 1e-30, None, ALU.max))
                tick(dve.tensor_scalar(FB, FB, 1e-30, None, ALU.max))
                dve.wait_ge(sig_done, 5)
                tick(dve.tensor_tensor(G, G, TT[:], ALU.mult))
                dve.wait_ge(kout_turned, 1)
                tick(dve.tensor_copy(QB, QF))
                dve.wait_ge(prep, 20)
                tick(dve.tensor_tensor(KS, KFW.rearrange("p h n -> p (h n)").rearrange("p (u t) -> p u t", u=UNITS),
                                       KBW.rearrange("p h n -> p (h n)").rearrange("p (u t) -> p u t", u=UNITS),
                                       ALU.add))
                for ht in range(4):
                    dve.wait_ge(cat_hi, ht + 1)
                    dve.tensor_tensor(HL[:, 4 + ht, :], BQ[:, ht, :], HH[:, 4 + ht, :].bitcast(F32),
                                      ALU.subtract).then_inc(cat_ready, 1)
                dve.wait_ge(kv_stored, 32)
                for cc in range(3):
                    dve.wait_ge(diag_mm, cc + 1)
                    dve.tensor_copy(ATT[:, 4 * cc:4 * cc + 4, :],
                                    bank[cc][:].rearrange("p (u t) -> p u t", u=4)).then_inc(diag_out, 1)
                tick(dve.tensor_tensor(QF, QF, FF, ALU.mult))
                tick(dve.tensor_tensor(QB, QB, FB, ALU.mult))
                assert n[0] == PREP, n
                for lv in range(LEVELS):
                    b = 1 << lv
                    for w in range(2):
                        q, f = (QF, QB)[w], (FF, FB)[w]
                        dve.wait_ge(lvl_mm, 2 * lv + w + 1)
                        if lv == 0:
                            dve.wait_ge(diag_out, 3)
                        out = ATT.rearrange("p u (m w i) -> p u m w i", w=2, i=b)[:, :, :, 1 - w, :]
                        for half in range(2):
                            if lv + w:
                                dve.wait_ge(lvl_out, 4 * lv + 2 * w + half - 1)
                            mask = LMASK[:, 2 * lv + w, :].rearrange("p (u m i) -> p u m i", u=1, i=b)
                            dve.copy_predicated(out[:, 6 * half:6 * half + 6],
                                                mask.broadcast_to([P, 6, P // (2 * b), b]),
                                                bank[3 + 2 * w + half][:, 0:6 * 64].rearrange(
                                                    "p (u m i) -> p u m i", u=6, i=b)).then_inc(lvl_out, 1)
                        if lv == 0:
                            dve.wait_ge(prep, PREP)
                        else:
                            dve.wait_ge(lvl_t, 2 * (lv - 1) + w + 1)
                        qh = halves(q, b)[:, :, 1 - w, :]
                        dve.tensor_tensor(qh, qh, total(f, b, w), ALU.mult).then_inc(lvl_q, 1)
                        dve.wait_ge(lvl_k, 2 * lv + w + 1)
                        dve.wait_ge(lvl_q, 2 * lv + w + 1)
                        tl, tr = halves(f, b)[:, :, 0, 0:1], halves(f, b)[:, :, 1, 0:1]
                        dve.tensor_tensor(tl, tl, tr, ALU.mult).then_inc(lvl_t, 1)
                for g in range(first_group("modC"), first_group("modD")):
                    coefficients(g)
                dve.wait_ge(state_landed, 16)
                dve.wait_ge(lvl_t, 2 * LEVELS)
                for h in range(HEADS_A):
                    dve.wait_ge(st_mm, h + 1)
                    B = bank[3 + h % 2]
                    for w in range(2):
                        k, f = (KFW, KBW)[w], (FF, FB)[w]
                        unit = 1 + w
                        dve.tensor_copy(k[:, h, 0:P], B[:, 256 * w:256 * w + P]).then_inc(st_ready, 1)
                        dve.scalar_tensor_tensor(k[:, h, P:2 * P], ST[:, 4 * w + h, :], f[:, h, unit * P:unit * P + 1],
                                                 B[:, 256 * w + P:256 * w + 256], ALU.mult, ALU.add) \
                            .then_inc(st_ready, 1)
                for h in range(HEADS_A):
                    dve.wait_ge(o_root, h + 1)
                    dve.reciprocal(RSTD[:], ROOT[:]).then_inc(o_step, 1)
                    dve.wait_ge(o_step, 4 * h + 1)
                    dve.tensor_tensor(FF[:, h, :], FF[:, h, :], RSTD[:], ALU.mult).then_inc(o_step, 1)
                    dve.wait_ge(o_step, 4 * h + 2)
                    dve.scalar_tensor_tensor(FF[:, h, :], FF[:, h, :], PAR[:, PAR_GN:PAR_GN + 1], G[:, h, :],
                                             ALU.mult, ALU.mult).then_inc(o_step, 1)
                    dve.wait_ge(cat_hi, 4 + h + 1)
                    dve.tensor_tensor(HL[:, h, :], FF[:, h, :], HH[:, h, :].bitcast(F32),
                                      ALU.subtract).then_inc(o_step, 1)
                for n_ in range(-2, 4):
                    for half in ahead(dve, split_dve, s, "out", n_):
                        half()
                    for b in range(2 if n_ >= 0 else 0):
                        add_square(s, 2 * n_ + b)

            def odd(s):
                for t in (CB, CG, U):
                    for at in (0, SEQ + 1, PADDED - 1):
                        x = dve.memset(t[:, :, at:at + 1], 0.0)
                x.then_inc(pads_set, 1)
                dve.wait_ge(pads_set, 1)
                for tau in range(24):
                    if tau % 2 == 0:
                        for half in ahead(dve, split_dve, s, "in", tau // 2):
                            half()
                    if tau < 16:
                        continue
                    d = tau - 16
                    dve.wait_ge(half_used, used(f"in{s}", tau // 2, tau % 2))
                    dve.wait_ge(proj_out, 32 + 8 + d + 1)
                    for g, (t0, t1) in enumerate(GROUPS):
                        x = dve.tensor_tensor(U[:, d % 2, t0 + 1 + g:t1 + 1 + g], bank[tau % 4][:, t0:t1],
                                              CG[:, d, t0 + 1 + g:t1 + 1 + g], ALU.mult)
                    x.then_inc(conv_step, 1)
                    dve.wait_ge(conv_step, 4 * d + 1)
                    if d:
                        dve.wait_ge(conv_done, d)
                    n = PADDED - 2
                    taps = [PAR[:, PAR_CONV + 8 * w + d:PAR_CONV + 8 * w + d + 1] for w in range(3)]
                    y = Y[:, 0:n]
                    dve.tensor_scalar(y, U[:, d % 2, 1:1 + n], taps[1], None, ALU.mult).then_inc(conv_step, 1)
                    for q, w in enumerate((0, 2)):
                        dve.wait_ge(conv_step, 4 * d + 2 + q)
                        dve.scalar_tensor_tensor(y, U[:, d % 2, w:w + n], taps[w], y, ALU.mult,
                                                 ALU.add).then_inc(conv_step, 1)
                    dve.wait_ge(conv_step, 4 * d + 4)
                    dve.wait_ge(proj_out, 32 + d + 1)
                    dve.tensor_tensor(CG[:, d, 1:1 + n], y, CB[:, d, 1:1 + n], ALU.mult).then_inc(conv_done, 1)
                for d in range(KD):
                    dve.wait_ge(cat_hi, 8 + d + 1)
                    dve.wait_ge(conv_done, KD)
                    for g, (t0, t1) in enumerate(GROUPS):
                        x = dve.tensor_tensor(HL[:, d, t0:t1], CG[:, d, t0 + 1 + g:t1 + 1 + g],
                                              HH[:, d, t0:t1].bitcast(F32), ALU.subtract)
                    x.then_inc(cat_ready, 1)
                for n in range(4):
                    for half in ahead(dve, split_dve, s, "out", n):
                        half()
                    for b in range(2):
                        add_square(s, 2 * n + b)

            coefficients(0)
            coefficients(1)
            pre(0)
            for s in range(upto):
                kind = SUBLAYERS[s][0]
                {"ffn": ffn, "even": even, "odd": odd}[kind](s)
                post(s, {"ffn": OUTF, "even": OUTM, "odd": OUTC}[kind])
                if s < upto - 1:
                    pre(s + 1)
            for t in range(TOKS):
                for b in range(2):
                    dve.wait_ge(tp_done, 9 + 2 * t + b + 1)
                    dve.tensor_copy(XS[:, t, b * 512:(b + 1) * 512], bank[(2 * t + b) % 4 + 4][:]) \
                        .then_inc(y_copied, 1)

        @block.tensor
        def _(pe):
            pe.sem_inc(half_used, 4)
            pe.wait_ge(setup_landed, 16 * 14)
            for t in range(3):
                n = min(P, PAR_ROWS - t * P)
                mm = pe.transpose(bank[0][:, t * P:t * P + n], PS[0:n, t, :], IDENT[0:n, 0:n])
            mm.then_inc(tp_done, 1)
            pe.wait_ge(x_landed, 48)
            for d in range(KD):
                if d >= 4:
                    pe.wait_ge(delta, (d - 4) // 2 + 1) if d % 2 == 0 else pe.wait_ge(x_ready, (d - 4) // 2 + 1)
                for t in range(TOKS):
                    mm = pe.transpose(bank[1 + d % 4][:, t * P:(t + 1) * P], XS[:, t, d * P:(d + 1) * P], IDENT[:])
                mm.then_inc(tp_done, 1)

            def mod_slot(st, n):
                k = 4 * first_group(st) + n
                g, q = divmod(k, 4)
                p, uses = ring_at(st, n)
                if q == 0 and g >= 2:
                    pe.wait_ge(mod_cols, g - 1)
                pe.wait_ge(raw_landed[p], 16 * (uses + 1))
                for kk in range(KD):
                    mm = pe.matmul(bank[MOD_BANK[g]][32 * q:32 * q + 32, 0:256], COND[:, kk, :],
                                   RAW[:, p, kk, :], start=(kk == 0), stop=(kk == KD - 1))
                mm.then_inc(mod_used, 1)

            def mod_turn(g):
                pick = IDENT[:].rearrange("p (q r) -> p q r", r=32)[:, :, 0:2]
                B = bank[MOD_BANK[g]]
                pe.wait_ge(mod_rows, g + 1)
                for h in range(2):
                    mm = pe.matmul(B[:, 8 * h:8 * h + 8].rearrange("p (q g) -> p q g", g=2),
                                   ROWS[:, h * P:(h + 1) * P], pick, start=True, stop=True)
                mm.then_inc(mod_turned, 1)

            def mod_stage(st):
                g0 = first_group(st)
                for n in range(stages[st]["n"]):
                    mod_slot(st, n)
                    if n >= 4 and n % 4 == 2:
                        mod_turn(g0 + n // 4 - 1)
                mod_turn(g0 + stages[st]["n"] // 4 - 1)

            def pre_stats(s):
                pe.wait_ge(const_set, 1)
                for pp in range(4):
                    pe.wait_ge(xsq_done, 4 * s + pp + 1)
                    for b in range(2):
                        src = SQ[:, b, :] if pp % 2 == 0 else TT[:, 2 + b, :]
                        mm = pe.matmul(cols3(bank[1]), ONES[:], src, start=(pp + b == 0), stop=(pp == 3 and b == 1))
                    mm.then_inc(stat_done, 1)

            def post_stats(s):
                pe.wait_ge(sq_added, 8 * s + 8)
                pe.matmul(cols3(bank[0]), ONES[:], ACC[:], start=True, stop=True).then_inc(stat_done, 1)

            def ffn(s):
                f, st = SUBLAYERS[s][1], f"in{s}"

                def pair(i, j):
                    base = 22 * f + j
                    for b in range(2):
                        pe.wait_ge(silu_done, i * 6 + (base + b + 1))
                        pe_half(pe, st, 2 * j + b, hh, hl, 8, cols3(bank[b]), True, True, i,
                                h_wait=8 * s if (j, b) == (0, 0) else None)
                    for b in range(2):
                        pe.wait_ge(gated, i * 6 + (base + b + 1))
                        pe_half(pe, st, 2 * j + 2 + b, hh, hl, 8, cols3(bank[2 + b]), True, True, i)

                ffn_pairs(pe, pair)
                if s == 0:
                    mod_stage("modA")
                pe.wait_ge(mod_cols, first_group(BUBBLE[s]) if s < 5 else 18)
                st = f"out{s}"

                def quarter_pair(i):
                    for j in range(6):
                        r = j % 3
                        for b in range(2):
                            t = 2 * (j // 3) + b
                            if r == 0:
                                pe.wait_ge(out_done, i * 4 + (8 * s + t + 1))
                            if b == 0:
                                pe.wait_ge(act_ready, 2 + 22 * f + min(8 * r + 8, KF))
                            pe_half(pe, st, 2 * j + b, lambda kk: AH[:, 8 * r + kk, :],
                                    lambda kk: AL[:, 8 * r + kk, :], out_nk(st, j), cols3(bank[4 + t]),
                                    r == 0, r == 2, i)

                with pe.Fori(0, 2) as i:
                    quarter_pair(i)

            def out_small(s):
                pe.wait_ge(mod_cols, first_group(BUBBLE[s]))
                for n in range(4):
                    for b in range(2):
                        d = 2 * n + b
                        pe.wait_ge(out_done, 8 * s + d + 1)
                        pe_half(pe, f"out{s}", d, hh, hl, 8, cols3(bank[4 + d % 4]), True, True)

            def even(s):
                def proj(tau):
                    if tau >= 4:
                        pe.wait_ge(proj_out, tau - 3)
                    part = AB_ORDER[tau // 2] // 2
                    if part not in (3, 7):
                        pe_half(pe, f"in{s}", tau, hh, hl, 8, cols3(bank[tau % 4]), True, True,
                                h_wait=8 * s if tau == 0 else None)
                        return
                    j = tau // 2
                    H = 2 * (stages[f"in{s}"]["m"] + j)
                    k = H % 4
                    pe.wait_ge(half_ready, H + 2)
                    for t in ((0, 1), (2,))[tau % 2]:
                        out = bank[tau % 4][:, (t % 2) * 256:(t % 2) * 256 + 256].rearrange("p (b n) -> p b n", b=2)
                        tok = slice(t * P, (t + 1) * P)
                        for kk in range(KD):
                            pe.matmul(out, HH[:, kk, tok], WH[:, k:k + 2, kk, :], start=(kk == 0), stop=False)
                            pe.matmul(out, HL[:, kk, tok], WH[:, k:k + 2, kk, :], start=False, stop=False)
                            mm = pe.matmul(out, HH[:, kk, tok], WL[:, k:k + 2, kk, :], start=False,
                                           stop=(kk == KD - 1))
                    if tau % 2:
                        mm.then_inc(half_used, 2)

                for tau in range(12):
                    proj(tau)
                pe.wait_ge(ctx_landed, 32)
                for ht in range(4):
                    mm = pe.transpose(bank[6][:, ht * P:(ht + 1) * P], CKR[:, ht * P:(ht + 1) * P], IDENT[:])
                mm.then_inc(ctx_turned, 1)
                pe.wait_ge(proj_out, 12)
                pe.wait_ge(ctx_ready, 1)
                filled = [0]
                g0 = first_group("modC")

                def fill(count):
                    for _ in range(count):
                        n = filled[0]
                        filled[0] += 1
                        mod_slot("modC", n)
                        if n % 4 == 2 and n // 4 not in (0, 3):
                            mod_turn(g0 + n // 4 - 1)

                for step in range(24 + 3):
                    u = step
                    if u < 24:
                        h, i = divmod(u, 3)
                        ht, pb = h // 2, DH * (h % 2)
                        S = bank[4 + u % 2]
                        if u >= 2:
                            pe.wait_ge(s_exp, u - 1)
                        q = BQ[pb:pb + DH, ht, i * P:(i + 1) * P]
                        if i == 0:
                            mm = pe.matmul(S[:, 0:P], q, BK[pb:pb + DH, ht, 0:P], start=True, stop=True)
                        else:
                            if i == 1:
                                pe.wait_ge(bias_ready, h + 1)
                            x0 = (2 - 2 * (i - 1)) * GRID_W
                            pe.matmul(S[:, 0:DEC_SEQ], q, BK[pb:pb + DH, ht, SEQ:NT], start=True, stop=False)
                            pe.matmul(S[:, 0:DEC_SEQ], FLIP[:], BIAS.rearrange("p a b -> p (a b)")
                                      [:, x0:x0 + DEC_SEQ], start=False, stop=True)
                            mm = pe.matmul(S[:, DEC_SEQ:NT], q, CKT[pb:pb + DH, ht, :], start=True, stop=True)
                        mm.then_inc(s_mm, 1)
                    u = step - 2
                    if 0 <= u < 24:
                        pe.wait_ge(p_ready, u + 1)
                        if u >= 1:
                            pe.wait_ge(p_copied, u)
                        for t in range(1 if u % 3 == 0 else 3):
                            mm = pe.transpose(bank[6][:, t * P:(t + 1) * P], TT[:, u % 4, t * P:(t + 1) * P], IDENT[:])
                        mm.then_inc(p_turned, 1)
                    u = step - 3
                    if 0 <= u < 24:
                        h, i = divmod(u, 3)
                        pb = DH * (h % 2)
                        out = bank[7][pb:pb + DH, i * P:(i + 1) * P]
                        pe.wait_ge(p_copied, u + 1)
                        if u % 6 == 0 and u:
                            pe.wait_ge(ob_done, u // 6)
                        vals = [BV[:, 0, h * DH:(h + 1) * DH]] if i == 0 else \
                            [BV[:, 1, h * DH:(h + 1) * DH], BV[:, 2, h * DH:(h + 1) * DH], CV[:, h, :]]
                        for t, v in enumerate(vals):
                            mm = pe.matmul(out, v, SQ[:, u % 2, t * P:(t + 1) * P], start=(t == 0),
                                           stop=(t == len(vals) - 1))
                        mm.then_inc(pv_done, 1)
                    if step < 20:
                        proj(12 + step)
                    else:
                        pe.wait_ge(proj_out, 32)
                        fill(1)
                for ht in range(4):
                    mm = pe.transpose(bank[6][:, ht * P:(ht + 1) * P], BK[:, ht, 0:P], IDENT[:])
                mm.then_inc(kout_turned, 1)

                def unit(t, u):
                    return t[:, u // TOKS, (u % TOKS) * P:(u % TOKS + 1) * P]

                fill(5)
                mod_turn(g0 + 2)
                pe.wait_ge(mod_cols, g0 + 3)
                pe.wait_ge(prep, 21)
                for u in range(UNITS):
                    mm = pe.matmul(bank[u // 4][:, (u % 4) * P:(u % 4 + 1) * P], KS[:, u, :], unit(QF, u),
                                   start=True, stop=True)
                    if u % 4 == 3:
                        mm.then_inc(diag_mm, 1)
                for lv in range(LEVELS):
                    b = 1 << lv
                    for w in range(2):
                        q, k = (QF, QB)[w], (KFW, KBW)[w]
                        if lv == 0:
                            pe.wait_ge(prep, PREP)
                        else:
                            pe.wait_ge(lvl_q, 2 * (lv - 1) + w + 1)
                            pe.wait_ge(lvl_k, 2 * (lv - 1) + w + 1)
                            pe.wait_ge(lvl_out, 4 * (lv - 1) + 2 * w + 2)
                        for u in range(UNITS):
                            rhs = unit(q, u).rearrange("p (m w i) -> p m w i", w=2, i=b)[:, :, 1 - w, :]
                            out = bank[3 + 2 * w + u // 6][:, (u % 6) * 64:(u % 6 + 1) * 64]
                            mm = pe.matmul(out.rearrange("p (m i) -> p m i", i=b), unit(k, u), rhs,
                                           start=True, stop=True)
                        mm.then_inc(lvl_mm, 1)
                        fill((2 if w else 1) + (w == 0 and lv < 3))
                assert filled[0] == stages["modC"]["n"]
                mod_turn(g0 + 8)
                pe.wait_ge(lvl_k, 2 * LEVELS)
                pe.wait_ge(lvl_out, 4 * LEVELS)
                for h in range(HEADS_A + 1):
                    if h < HEADS_A:
                        if h >= 1:
                            pe.wait_ge(k_copied, h)
                        for j, (k, blk) in enumerate(((KFW, 0), (KFW, 1), (KBW, 0), (KBW, 2))):
                            mm = pe.transpose(bank[5][:, j * P:(j + 1) * P], k[:, h, blk * P:(blk + 1) * P], IDENT[:])
                        mm.then_inc(k_turned, 1)
                    g = h - 1
                    if g >= 0:
                        pe.wait_ge(k_copied, g + 1)
                        if g >= 2:
                            pe.wait_ge(st_ready, 4 * (g - 1))
                        for j, blk in enumerate((0, 1, 0, 2)):
                            mm = pe.matmul(bank[3 + g % 2][:, j * P:(j + 1) * P], KTOK[:, g % 2, j, :],
                                           VT[:, blk, g * P:(g + 1) * P], start=True, stop=True)
                        mm.then_inc(st_mm, 1)
                pe.wait_ge(mod_cols, first_group("modD"))
                for h in range(HEADS_A):
                    pe.wait_ge(st_ready, 4 * h + 4)
                    O = bank[OB[h]]
                    for t in range(TOKS):
                        out = O[:, t * P:(t + 1) * P]
                        terms = [(VT[:, t, h * P:(h + 1) * P], ATT[:, TOKS * h + t, :])]
                        if t > 0:
                            first = (ST[:, h, :], KFW[:, h, P:2 * P])
                            last = (ST[:, 4 + h, :], KBW[:, h, P:2 * P])
                            terms.append((first[t - 1], QF[:, h, t * P:(t + 1) * P]))
                            terms.append((last[2 - t], QB[:, h, t * P:(t + 1) * P]))
                        for n, (l, r) in enumerate(terms):
                            mm = pe.matmul(out, l, r, start=(n == 0), stop=(n == len(terms) - 1))
                    mm.then_inc(o_mm, 1)
                for h in range(HEADS_A):
                    pe.wait_ge(o_sq, h + 1)
                    if h >= 2:
                        pe.wait_ge(o_root, h - 1)
                    pe.matmul(cols3(bank[(6, 3)[h % 2]]), ONES[:], SQ[:, h % 2, :], start=True, stop=True) \
                        .then_inc(o_stat, 1)
                pe.wait_ge(cat_ready, 4)
                pe.wait_ge(o_step, 16)
                out_small(s)

            def odd(s):
                for tau in range(24):
                    if tau >= 20:
                        pe.wait_ge(conv_step, 4 * (tau - 20) + 1)
                    elif tau >= 4:
                        pe.wait_ge(proj_out, 32 + tau - 3)
                    pe_half(pe, f"in{s}", tau, hh, hl, 8, cols3(bank[tau % 4]), True, True,
                            h_wait=8 * s if tau == 0 else None)
                pe.wait_ge(cat_ready, 4 + KD)
                out_small(s)

            pe.sem_inc(silu_done, 2)
            pe.sem_inc(out_done, 4)
            pe.wait_ge(cond_ready, 1)
            pe.wait_ge(x_ready, 4)
            mod_stage("mod0")
            pre_stats(0)
            for s in range(upto):
                {"ffn": ffn, "even": even, "odd": odd}[SUBLAYERS[s][0]](s)
                post_stats(s)
                if s < upto - 1:
                    pe.wait_ge(out_done, 4 + 8 * (s + 1))
                    for n in range(4):
                        mod_slot(BUBBLE[s], n)
                    pre_stats(s + 1)
                    mod_turn(first_group(BUBBLE[s]))
            pe.wait_ge(x_ready, 4 * upto + 4)
            for t in range(TOKS):
                for b in range(2):
                    if 2 * t + b >= 4:
                        pe.wait_ge(y_copied, 2 * t + b - 3)
                    for d in range(4):
                        mm = pe.transpose(bank[(2 * t + b) % 4 + 4][:, d * P:(d + 1) * P],
                                          X[:, 4 * b + d, t * P:(t + 1) * P], IDENT[:])
                    mm.then_inc(tp_done, 1)


_INS = ['x_prompt', 'x_sample', 'c', 'state_hgrn', 'cache_k', 'cache_v', 'c_ctx', 'mod_w', 'mod_b', 'norm_pre',
        'norm_post', 'ffn_w_in', 'ffn_w_out', 'ab_w_in', 'ab_w_out', 'a_lb', 'a_gnorm', 'b_rpb', 'cv_w_in',
        'cv_conv', 'cv_w_out']
_OUTS = [(1, 128, 1024), (1, 256, 1024), (1, 1, 2, 4, 128, 128), (1, 1, 8, 128, 64), (1, 1, 8, 128, 64)]


def kernel(**inputs):
    import concourse.bacc as bacc
    from concourse.bass_utils import run_bass_kernel_spmd

    nc = bacc.Bacc("TRN2", target_bir_lowering=False, num_devices=1)
    arrays, args = {}, []
    given = {name: np.ascontiguousarray(inputs[name]) for name in _INS}
    given |= dict(zip(("identity", "level_masks", "window_mask", "flip_scaled"), constants()))
    for name, a in given.items():
        arrays[f"in_{name}"] = a
        args.append(nc.dram_tensor(f"in_{name}", a.shape, mybir.dt.from_np(a.dtype), kind="ExternalInput").ap())
    for i, shape in enumerate(_OUTS):
        args.append(nc.dram_tensor(f"out_{i}", shape, F32, kind="ExternalOutput").ap())
    trunk(nc, *args)
    r = run_bass_kernel_spmd(nc, [arrays], core_ids=[0])
    return tuple(r.results[0][f"out_{i}"] for i in range(len(_OUTS)))
```

```python
from contextlib import ExitStack

import numpy as np

import concourse.bass as bass
from concourse import mybir

P = 128
D_MODEL, SEQ, DEC_SEQ, DEPTH = 1024, 128, 256, 2
NT = SEQ + DEC_SEQ
GROUPS = ((0, SEQ), (SEQ, NT))
KD = D_MODEL // P
D_FF = 2816
KF = D_FF // P
D_A = D_MODEL // 2
HEADS_A, HEADS_B, DH = 4, 8, 64
AB_IN = 8 * D_A
GRID_W, NA_COLS, NA_ROWS, ROWS = 64, 16, 8, DEC_SEQ // 64
RPB_W, RPB_H = 2 * NA_COLS - 1, 2 * NA_ROWS - 1
TOKS = NT // P
UNITS = HEADS_A * TOKS
EPS = 1e-6
LB_MAX = 1.0 - 1e-4
LEVELS = 7
PADDED = NT + 3
RING = 6
NEG = -1e30

F32 = mybir.dt.float32
F32R = mybir.dt.float32r
I32 = mybir.dt.int32
ALU = mybir.AluOpType
ACT = mybir.ActivationFunctionType
AX = mybir.AxisListType

PAR_MOD, PAR_PRE, PAR_POST, PAR_CONV, PAR_LB, PAR_GN, PAR_COND = 0, 144, 192, 240, 264, 272, 273
PAR_ROWS = 289

SUBLAYERS = (("ffn", 0), ("even", 0), ("ffn", 1), ("ffn", 2), ("odd", 0), ("ffn", 3))
HALF = (0.5, 1.0, 0.5, 0.5, 1.0, 0.5)


MIDDLE = ("modA", "modC", "modE", "modG", "modI")
BETWEEN = ("modB", "modD", "modF", "modH", "modJ")
MOD_GROUPS = {"mod0": 2, "modA": 1, "modB": 2, "modC": 6, "modD": 1, "modE": 1, "modF": 1, "modG": 1, "modH": 1,
              "modI": 1, "modJ": 1}


def first_group(st):
    names = list(MOD_GROUPS)
    return sum(MOD_GROUPS[n] for n in names[:names.index(st)])


MOD_BANK = [7 - g % 2 for g in range(18)]
MOD_BANK[5:11] = [3, 2, 3, 7, 2, 7]


def between(s):
    st = BETWEEN[s - 1]
    return [first_group(st) + n for n in range(MOD_GROUPS[st])] if s else []


def constants():
    s = np.arange(P)[:, None]
    c = np.arange(P // 2)[None, :]
    masks = np.zeros((P, 2 * LEVELS, P // 2), np.int32)
    for lv in range(LEVELS):
        b = 1 << lv
        same = (s // (2 * b)) == (c // b)
        masks[:, 2 * lv] = same & ((s // b) % 2 == 0)
        masks[:, 2 * lv + 1] = same & ((s // b) % 2 == 1)
    q = np.arange(P) % GRID_W
    c0 = np.clip(q - NA_COLS // 2, 0, GRID_W - NA_COLS)[:, None]
    k = np.arange(GRID_W)[None, :]
    window = np.where((k >= c0) & (k < c0 + NA_COLS), 0.0, NEG).astype(np.float32)
    order = np.concatenate([np.arange(64)[::-1], 64 + np.arange(64)[::-1]])
    flip = np.zeros((P, P), np.float32)
    flip[order, np.arange(P)] = DH ** 0.5
    return np.eye(P, dtype=np.float32), masks, window[order], flip


def plan():
    stages, slot, split, mod = {}, 0, 0, 0
    kinds = []

    def add(name, n, kind):
        nonlocal slot, split, mod
        stages[name] = dict(a=slot, m=split, q=mod, n=n)
        slot += n
        for _ in range(n):
            if kind == "split":
                split += 1
            else:
                mod += 1
            kinds.append((kind, split, mod))

    add("mod0", 4 * MOD_GROUPS["mod0"], "mod")
    for s, (kind, _) in enumerate(SUBLAYERS):
        add(f"in{s}", {"ffn": 22, "even": 16, "odd": 12}[kind], "split")
        if s < 5:
            add(MIDDLE[s], 4 * MOD_GROUPS[MIDDLE[s]], "mod")
        add(f"out{s}", {"ffn": 12, "even": 4, "odd": 4}[kind], "split")
        if s < 5:
            add(BETWEEN[s], 4 * MOD_GROUPS[BETWEEN[s]], "mod")
    return stages, kinds


def trunk(nc, x_prompt, x_sample, c, state_hgrn, cache_k, cache_v, c_ctx, mod_w, mod_b, norm_pre, norm_post,
          ffn_w_in, ffn_w_out, ab_w_in, ab_w_out, a_lb, a_gnorm, b_rpb, cv_w_in, cv_conv, cv_w_out,
          identity, level_masks, window_mask, flip_scaled,
          y_prompt, y_sample, state_new, cache_k_new, cache_v_new, upto=6):
    stages, kinds = plan()
    ctx = ExitStack()
    with ctx:
        def sb(name, shape, dt=F32):
            return ctx.enter_context(nc.sbuf_tensor(name, shape, dt))

        def sem(name):
            return ctx.enter_context(nc.semaphore(name))

        X = sb("X", [P, KD, NT])
        RAW = sb("RAW", [P, RING, 8, 256])
        WH = sb("WH", [P, 4, 8, P], F32R)
        WL = sb("WL", [P, 4, 8, P], F32R)
        TT = sb("TT", [P, 4, NT])
        SQ = sb("SQ", [P, 2, NT])
        ACC = sb("ACC", [P, NT])
        ROOT = sb("ROOT", [P, NT])
        RSTD = sb("RSTD", [P, NT])
        IDENT = sb("IDENT", [P, P])
        ONES = sb("ONES", [P, P])
        LMASK = sb("LMASK", [P, 2 * LEVELS, P // 2], I32)
        WINDOW = sb("WINDOW", [P, GRID_W])
        FLIP = sb("FLIP", [P, P])
        PAR = sb("PAR", [P, NT])
        COND = sb("COND", [P, KD, 32])
        ROWS = sb("ROWS", [P, 256])
        MOD = sb("MOD", [P, 144, 2])
        CA = sb("CA", [P, 6, KD, 2])
        CC = sb("CC", [P, 6, KD, 2])
        LBT = sb("LBT", [P, 4, 8])
        SMALL = sb("SMALL", [P, 3, 4])
        EPSC = sb("EPSC", [P, 1])
        with nc.sbuf_tensor("OUTF", [P, KD, NT], F32) as OUTF:
            pass
        HH = sb("HH", [P, KD, NT], F32R)
        HL = sb("HL", [P, KD, NT], F32R)
        MIX_WORDS = 17152
        with nc.sbuf_tensor("AH", [P, KF, NT], F32R) as AH:
            with nc.sbuf_tensor("AL", [P, KF, NT], F32R) as AL:
                pass
        MIX = sb("MIX", [P, MIX_WORDS])

        def mix(at, *shape):
            n = int(np.prod(shape))
            v = MIX[:, at:at + n]
            if len(shape) == 2:
                return v.rearrange("p (a b) -> p a b", a=shape[0])
            if len(shape) == 3:
                return v.rearrange("p (a b c) -> p a b c", a=shape[0], b=shape[1])
            return v

        W15 = 4 * NT
        BQ, BK, BV = mix(0, 4, NT), mix(W15, 4, NT), mix(2 * W15, TOKS, 512)
        BIAS = mix(3 * W15, 6, GRID_W)
        CKT, CV = mix(3 * W15 + 384, 4, P), mix(3 * W15 + 896, HEADS_B, DH)
        AT0 = 3 * W15 + 1408
        QF, KFW, FF, FB, KBW, V, G = (mix(AT0 + i * W15, 4, NT) for i in range(7))
        VT = mix(AT0 + 5 * W15, TOKS, 512)
        CKR = TT[:, :, :].rearrange("p a b -> p (a b)")[:, 0:512]
        QB = BK
        ATT = mix(2 * W15, UNITS, P)
        ST = mix(3 * W15 + 384, 8, P)
        OUTM = mix(AT0 + 2 * W15, KD, NT)
        KS = TT[:, :, :].rearrange("p a b -> p (a b)").rearrange("p (u t) -> p u t", u=UNITS)
        KTOK = TT[:, :, :].rearrange("p a b -> p (a b)")[:, 0:1024].rearrange("p (h j t) -> p h j t", h=2, j=4)
        KOUT = SQ[:, :, :].rearrange("p a b -> p (a b)")[:, 0:512]
        CB, CG = mix(0, KD, PADDED), mix(KD * PADDED, KD, PADDED)
        U = mix(2 * KD * PADDED, 2, PADDED)
        Y = mix((2 * KD + 2) * PADDED, PADDED)
        OUTC = mix((2 * KD + 3) * PADDED + 1, KD, NT)
        XS = mix(0, TOKS, D_MODEL)
        PS = TT[:, 0:1, :].rearrange("p a (t n) -> p (a t) n", t=3)

        bank = [ctx.enter_context(nc.psum_tensor(f"bank{i}", [P, 512], F32)) for i in range(8)]

        raw_landed = [sem(f"raw_landed{i}") for i in range(RING)]
        setup_landed = sem("setup_landed")
        x_landed = sem("x_landed")
        half_hi = sem("half_hi")
        half_ready = sem("half_ready")
        half_used = sem("half_used")
        mod_used = sem("mod_used")
        mod_rows = sem("mod_rows")
        mod_turned = sem("mod_turned")
        mod_cols = sem("mod_cols")
        coef_ready = sem("coef_ready")
        coef_step = sem("coef_step")
        tp_done = sem("tp_done")
        par_ready = sem("par_ready")
        cond_ready = sem("cond_ready")
        lb_step = sem("lb_step")
        const_set = sem("const_set")
        x_ready = sem("x_ready")
        xsq_done = sem("xsq_done")
        stat_done = sem("stat_done")
        root_done = sem("root_done")
        rstd_done = sem("rstd_done")
        h_scaled = sem("h_scaled")
        h_full = sem("h_full")
        h_hi = sem("h_hi")
        h_ready = sem("h_ready")
        silu_done = sem("silu_done")
        gated = sem("gated")
        act_hi = sem("act_hi")
        act_ready = sem("act_ready")
        out_sq = sem("out_sq")
        out_done = sem("out_done")
        sq_added = sem("sq_added")
        delta = sem("delta")
        out_scaled = sem("out_scaled")
        proj_out = sem("proj_out")
        ctx_landed, ctx_turned, ctx_ready = sem("ctx_landed"), sem("ctx_turned"), sem("ctx_ready")
        bias_landed, bias_ready = sem("bias_landed"), sem("bias_ready")
        s_mm, s_max, s_exp = sem("s_mm"), sem("s_max"), sem("s_exp")
        p_inv, p_ready, p_turned, p_copied = sem("p_inv"), sem("p_ready"), sem("p_turned"), sem("p_copied")
        pv_done, ob_done = sem("pv_done"), sem("ob_done")
        kout_turned, kout_ready, kv_stored = sem("kout_turned"), sem("kout_ready"), sem("kv_stored")
        cat_hi, cat_ready = sem("cat_hi"), sem("cat_ready")
        sig_done, prep = sem("sig_done"), sem("prep")
        k_scaled = sem("k_scaled")
        diag_mm, diag_out = sem("diag_mm"), sem("diag_out")
        lvl_mm, lvl_out, lvl_q, lvl_k, lvl_t = (sem(n) for n in ("lvl_mm", "lvl_out", "lvl_q", "lvl_k", "lvl_t"))
        state_landed, state_stored = sem("state_landed"), sem("state_stored")
        k_turned, k_copied, st_mm, st_ready = sem("k_turned"), sem("k_copied"), sem("st_mm"), sem("st_ready")
        o_mm, o_sq, o_copied, o_stat, o_root = (sem(n) for n in ("o_mm", "o_sq", "o_copied", "o_stat", "o_root"))
        o_step = sem("o_step")
        g_ready = sem("g_ready")
        pads_set, conv_step, conv_done = sem("pads_set"), sem("conv_step"), sem("conv_done")
        y_copied, y_stored = sem("y_copied"), sem("y_stored")

        def ring_at(st, j):
            return (stages[st]["a"] + j) % RING, (stages[st]["a"] + j) // RING

        def src_of(st, n):
            def cols(w, col, k0=0, k1=8):
                return w.rearrange("(k p) n -> p k n", p=P)[:, k0:k1, bass.ds(col, 256)]
            if st.startswith("mod"):
                t = 8 * first_group(st) + 2 * n
                return cols(mod_w[t // 72], (t % 72) * P), 8
            s = int(st[-1])
            kind, f = SUBLAYERS[s]
            if kind == "ffn":
                if st.startswith("in"):
                    return cols(ffn_w_in[f // 2, f % 2], (n // 2) * 256 + (n % 2) * D_FF), 8
                q, r = divmod(n, 3)
                return cols(ffn_w_out[f // 2, f % 2], q * 256, 8 * r, min(8 * r + 8, KF)), min(8, KF - 8 * r)
            if kind == "even":
                if st.startswith("in"):
                    return cols(ab_w_in[0], AB_ORDER[n] * 256), 8
                return cols(ab_w_out[0], n * 256), 8
            return cols((cv_w_in if st.startswith("in") else cv_w_out)[0], n * 256), 8

        AB_ORDER = [10, 11, 14, 15, 12, 13, 0, 1, 6, 7, 2, 3, 4, 5, 8, 9]

        def used(st, n, b):
            return 4 + 2 * (stages[st]["m"] + n) + b + 1

        def split_act(e, st, jj, nk, i=0):
            yield_b = []
            p, uses = ring_at(st, jj)
            m = stages[st]["m"] + jj
            for b in range(2):
                def half(b=b):
                    if b == 0:
                        e.wait_ge(raw_landed[p], (i + uses + 1) * 16)
                    e.wait_ge(half_used, i * 12 + (2 * m + b + 1))
                    e.activation(WH[:, (2 * m + b) % 4, 0:nk, :], RAW[:, p, 0:nk, b * P:(b + 1) * P],
                                 ACT.Copy).then_inc(half_hi, 1)
                yield_b.append(half)
            return yield_b

        def split_dve(e, st, jj, nk, i=0):
            out = []
            p, _ = ring_at(st, jj)
            m = stages[st]["m"] + jj
            for b in range(2):
                def half(b=b):
                    k = (2 * m + b) % 4
                    e.wait_ge(half_hi, i * 12 + (2 * m + b + 1))
                    e.tensor_tensor(WL[:, k, 0:nk, :], RAW[:, p, 0:nk, b * P:(b + 1) * P],
                                    WH[:, k, 0:nk, :].bitcast(F32), ALU.subtract).then_inc(half_ready, 1)
                out.append(half)
            return out

        def out_nk(st, n):
            kind = SUBLAYERS[int(st[-1])][0]
            return min(8, KF - 8 * (n % 3)) if kind == "ffn" and st.startswith("out") else 8

        def ahead(e, split, s, part, n):
            st, n2 = f"{part}{s}", n + 2
            if n2 >= stages[st]["n"]:
                if part == "out" or SUBLAYERS[s][0] == "even":
                    return [lambda: None] * 2
                st, n2 = f"out{s}", n2 - stages[st]["n"]
            return split(e, st, n2, out_nk(st, n2))

        def ffn_pairs(e, body):
            body(0, 0)
            with e.Fori(0, 3) as i:
                for j in (2, 4, 6):
                    body(i, j)
            body(0, 20)

        def pe_half(e, st, jj, xh, xl, nk, out, first, last, i=0):
            H = 2 * stages[st]["m"] + jj
            e.wait_ge(half_ready, i * 12 + (H + 1))
            k = H % 4
            for kk in range(nk):
                e.matmul(out, WH[:, k, kk, :], xh(kk), start=(first and kk == 0), stop=False)
                e.matmul(out, WH[:, k, kk, :], xl(kk), start=False, stop=False)
                mm = e.matmul(out, WL[:, k, kk, :], xh(kk), start=False, stop=(last and kk == nk - 1))
            mm.then_inc(half_used, 1)

        def pe_four(e, st, outs, order, ready):
            H = 2 * stages[st]["m"]
            e.wait_ge(half_ready, H + 4)
            for n, kk in enumerate(order):
                ready(kk)
                first, last = n == 0, n == len(order) - 1
                for b in range(4):
                    k = (H + b) % 4
                    e.matmul(outs[b], WH[:, k, kk, :], HH[:, kk, :], start=first, stop=False)
                    e.matmul(outs[b], WH[:, k, kk, :], HL[:, kk, :], start=False, stop=False)
                    mm = e.matmul(outs[b], WL[:, k, kk, :], HH[:, kk, :], start=False, stop=last)
                    if last:
                        mm.then_inc(half_used, 1)
                yield

        def cols3(t):
            return t[:, 0:NT]

        hh = lambda kk: HH[:, kk, :]
        hl = lambda kk: HL[:, kk, :]

        def halves(t, b):
            return t.rearrange("p h n -> p (h n)").rearrange("p (m w i) -> p m w i", w=2, i=b)

        def total(t, b, side):
            v = halves(t, b)[:, :, side, 0:1]
            return v.broadcast_to([P, UNITS * P // (2 * b), b])

        PREP = 17

        block = ctx.enter_context(nc.Block())

        @block.sync
        def _(sp):
            xr = [x_prompt[0], x_sample[0, 0:P], x_sample[0, P:2 * P]]
            for t in range(TOKS):
                sp.dma_start(XS[:, t, :], xr[t]).then_inc(x_landed, 16)
            sp.dma_start(IDENT[:], identity).then_inc(setup_landed, 16)
            rows = [(PAR_MOD, mod_b.rearrange("l (t p) -> (l t) p", p=P)),
                    (PAR_PRE, norm_pre.rearrange("l j (t p) -> (l j t) p", p=P)),
                    (PAR_POST, norm_post.rearrange("l j (t p) -> (l j t) p", p=P)),
                    (PAR_CONV, cv_conv.rearrange("o w (t p) -> (o w t) p", p=P)),
                    (PAR_LB, a_lb.rearrange("o w (t p) -> (o w t) p", p=P)),
                    (PAR_GN, a_gnorm),
                    (PAR_COND, c_ctx.rearrange("(t p) -> t p", p=P)),
                    (PAR_COND + 8, c[0].rearrange("(t p) -> t p", p=P))]
            n_par = 0
            for r0, src in rows:
                done, n = 0, src.shape[0]
                while done < n:
                    tile, at = divmod(r0 + done, P)
                    k = min(n - done, P - at)
                    sp.dma_start(PS[at:at + k, tile, :], src[done:done + k, :]).then_inc(setup_landed, 16)
                    done += k
                    n_par += 1
            assert n_par == 10, n_par
            sp.dma_start(LMASK[:], level_masks).then_inc(setup_landed, 16)
            sp.dma_start(WINDOW[:], window_mask).then_inc(setup_landed, 16)
            sp.dma_start(FLIP[:], flip_scaled).then_inc(setup_landed, 16)

            def load(st, jj, src, nk, i=0):
                p, _ = ring_at(st, jj)
                return sp.dma_start(RAW[:, p, 0:nk, :], src).then_inc(raw_landed[p], 16)

            def wait_ring(g):
                if g >= RING:
                    kind, m, q = kinds[g - RING]
                    if kind == "split":
                        sp.wait_ge(half_ready, 2 * m)
                    else:
                        sp.wait_ge(mod_used, q)

            for st, d in stages.items():
                if not st.startswith("mod") and int(st[-1]) >= upto or st == BETWEEN[min(upto, 5) - 1] and upto < 6:
                    break
                if st.startswith("in") and SUBLAYERS[int(st[-1])][0] == "ffn":
                    for n in range(RING):
                        wait_ring(d["a"] + n)
                        load(st, n, *src_of(st, n))
                    w = ffn_w_in[SUBLAYERS[int(st[-1])][1] // 2, SUBLAYERS[int(st[-1])][1] % 2]
                    w = w.rearrange("(k p) n -> p k n", p=P)
                    with sp.Fori(0, 2) as i:
                        for j in range(RING):
                            sp.wait_ge(half_ready, i * 12 + 2 * (d["m"] + j + 1))
                            col = i * 768 + (768 + (j // 2) * 256 + (j % 2) * D_FF)
                            load(st, j, w[:, :, bass.ds(col, 256)], 8)
                    for n in range(18, 22):
                        wait_ring(d["a"] + n)
                        load(st, n, *src_of(st, n))
                else:
                    for n in range(d["n"]):
                        wait_ring(d["a"] + n)
                        load(st, n, *src_of(st, n))

        @block.gpsimd
        def _(pool):
            pool.memset(ONES[:], 1.0)
            pool.memset(COND[:], 0.0)
            pool.memset(EPSC[:], EPS).then_inc(const_set, 1)

            def first_splits(st):
                pool.wait_ge(half_ready, 2 * stages[st]["m"])
                for n in range(2):
                    for half in split_dve(pool, st, n, 8):
                        half()

            def scale_out(s, OUT):
                pool.wait_ge(rstd_done, 2 * s + 2)
                pool.wait_ge(out_done, 4 + 8 * (s + 1))
                for pp in (2, 3):
                    o = OUT[:, 2 * pp:2 * pp + 2, :]
                    pool.tensor_tensor(o, o, RSTD[:].rearrange("p (a n) -> p a n", a=1).broadcast_to([P, 2, NT]),
                                       ALU.mult).then_inc(out_scaled, 1)

            first_splits("in0")
            scale_out(0, OUTF)
            if upto < 2:
                return
            first_splits("in1")
            pool.wait_ge(setup_landed, 16 * 14)
            pool.wait_ge(h_ready, 16)
            pool.dma_start(CKR, cache_k[0, 0].rearrange("h t d -> t h d")).then_inc(ctx_landed, 16)
            pool.dma_start(CV, cache_v[0, 0].rearrange("h t d -> t h d")).then_inc(ctx_landed, 16)
            for h in range(HEADS_B):
                if h >= 1:
                    pool.wait_ge(s_mm, 3 * h)
                for j in range(2):
                    off = h * RPB_H * RPB_W + (5 - j) * RPB_W + NA_COLS - 1 - (GRID_W - 1)
                    pool.dma_start(BIAS[64 * j:64 * j + 64], bass.AP(
                        tensor=b_rpb.tensor, offset=b_rpb.offset + off,
                        ap=[[1, GRID_W], [RPB_W, 6], [1, GRID_W]])).then_inc(bias_landed, 16)
                pool.wait_ge(bias_landed, 32 * (h + 1))
                pool.tensor_tensor(BIAS, BIAS, WINDOW[:].rearrange("p (a b) -> p a b", a=1)
                                   .broadcast_to([P, 6, GRID_W]), ALU.add).then_inc(bias_ready, 1)
            pool.wait_ge(pv_done, 24)
            pool.dma_start(ST, state_hgrn[0, 0].rearrange("w h k v -> k (w h) v")).then_inc(state_landed, 16)
            pool.wait_ge(sig_done, 1)
            for h in range(HEADS_A):
                pool.tensor_scalar(KFW[:, h, :], KFW[:, h, :], LBT[:, 3, h:h + 1], None,
                                   ALU.mult).then_inc(k_scaled, 1)
            for lv in range(LEVELS):
                b = 1 << lv
                for w in range(2):
                    pool.wait_ge(lvl_mm, 2 * lv + w + 1)
                    if lv == 0:
                        pool.wait_ge(prep, PREP)
                    else:
                        pool.wait_ge(lvl_t, 2 * (lv - 1) + w + 1)
                    k = halves((KFW, KBW)[w], b)[:, :, w, :]
                    pool.tensor_tensor(k, k, total((FF, FB)[w], b, 1 - w), ALU.mult).then_inc(lvl_k, 1)
            first_splits("out1")
            for s in range(1, upto):
                scale_out(s, {"ffn": OUTF, "even": OUTM, "odd": OUTC}[SUBLAYERS[s][0]])
                if s + 1 < upto:
                    first_splits(f"in{s + 1}")

        @block.scalar
        def _(act):
            act.wait_ge(par_ready, 1)
            act.wait_ge(const_set, 1)
            act.activation(COND[:, :, 0:2], PAR[:, PAR_COND:PAR_COND + 16].rearrange("p (g k) -> p k g", g=2),
                           ACT.Silu).then_inc(cond_ready, 1)
            act.wait_ge(lb_step, 1)
            act.activation(LBT[:, 0, :], LBT[:, 1, :], ACT.Exp).then_inc(lb_step, 1)

            def mod_rows_out(g):
                B = bank[MOD_BANK[g]]
                act.wait_ge(mod_used, 4 * g + 4)
                if g >= 1:
                    act.wait_ge(mod_turned, g)
                act.activation(ROWS[:], B[:, 0:256], ACT.Copy).then_inc(mod_rows, 1)

            def mod_cols_out(g):
                B = bank[MOD_BANK[g]]
                act.wait_ge(mod_turned, g + 1)
                act.activation(MOD[:, 8 * g:8 * g + 8, :].rearrange("p (q h) g -> p h q g", h=2),
                               B[:, 0:16].rearrange("p (h q g) -> p h q g", h=2, q=4),
                               ACT.Copy).then_inc(mod_cols, 1)

            def root(src, n_in, when):
                act.wait_ge(*when)
                act.activation(ROOT[:], cols3(src), ACT.Sqrt, bias=EPSC[:, 0:1],
                               scale=1.0 / n_in).then_inc(root_done, 1)

            def pre(s):
                groups = between(s)
                for pp in range(4):
                    act.wait_ge(x_ready, 4 * s + pp + 1)
                    if pp >= 2:
                        act.wait_ge(stat_done, 5 * s + pp - 1)
                    act.activation(SQ[:] if pp % 2 == 0 else TT[:, 2:4, :], X[:, 2 * pp:2 * pp + 2, :],
                                   ACT.Square).then_inc(xsq_done, 1)
                    split_act(act, f"in{s}", pp // 2, 8)[pp % 2]()
                    if pp == 1 and len(groups) == 2:
                        mod_rows_out(groups[0])
                if s:
                    mod_rows_out(groups[-1])
                root(bank[1], D_MODEL, (stat_done, 5 * s + 4))
                for g in groups:
                    mod_cols_out(g)
                act.wait_ge(coef_ready, 3 * s + 2)
                for d in range(KD):
                    act.wait_ge(h_scaled, 8 * s + d + 1)
                    for g, (t0, t1) in enumerate(GROUPS):
                        a = act.activation(HH[:, d, t0:t1], TT[:, d % 2, t0:t1], ACT.Identity,
                                           bias=MOD[:, 24 * s + d, g:g + 1], scale=CA[:, s, d, g:g + 1])
                    a.then_inc(h_hi, 1)

            def out_tile(s, OUT, st, n, b, d):
                act.wait_ge(half_used, used(st, n, b))
                if d >= 2:
                    act.wait_ge(sq_added, 8 * s + d - 1)
                act.activation(SQ[:, d % 2, :], cols3(bank[4 + d % 4]), ACT.Square).then_inc(out_sq, 1)
                if d == 0:
                    act.wait_ge(coef_ready, 3 * s + 3)
                for g, (t0, t1) in enumerate(GROUPS):
                    a = act.activation(OUT[:, d, t0:t1], bank[4 + d % 4][:, t0:t1], ACT.Copy,
                                       scale=CC[:, s, d, g:g + 1])
                a.then_inc(out_done, 1)

            def post(s):
                root(bank[0], D_MODEL, (stat_done, 5 * s + 5))

            def ffn(s):
                f, st = SUBLAYERS[s][1], f"in{s}"

                def pair(i, j):
                    nxt = [split_act(act, st, j + 2 + q, 8, i) for q in range(2)] if j < 20 else \
                        [split_act(act, f"out{s}", q, 8) for q in range(2)]
                    base = 22 * f + j
                    for b in range(2):
                        nxt[0][b]()
                        act.wait_ge(half_used, i * 12 + used(st, j, b))
                        act.wait_ge(gated, i * 6 + (base + b + 1))
                        act.activation(TT[:, b, :], cols3(bank[b]), ACT.Silu).then_inc(silu_done, 1)
                    nxt[1][0]()
                    nxt[1][1]()
                    for b in range(2):
                        act.wait_ge(gated, i * 6 + (2 + base + b + 1))
                        act.activation(AH[:, bass.ds(i * 6 + (j + b), 1), :], TT[:, 2 + b:3 + b, :],
                                       ACT.Copy).then_inc(act_hi, 1)

                ffn_pairs(act, pair)
                if s < 5:
                    mod_rows_out(first_group(MIDDLE[s]))
                    mod_cols_out(first_group(MIDDLE[s]))
                for n in range(12):
                    for half in ahead(act, split_act, s, "out", n):
                        half()
                    if n % 3 == 2:
                        for b in range(2):
                            out_tile(s, OUTF, f"out{s}", n, b, 2 * (n // 3) + b)

            def even(s):
                def proj(tau):
                    part, q = divmod(AB_ORDER[tau // 2] * 2 + tau % 2, 4)
                    halves_ahead = ahead(act, split_act, s, "in", tau // 2)
                    if part in (3, 7):
                        if tau % 2 == 0:
                            return
                        dst = (VT if part == 3 else BV)[:, :, (q // 2) * 256:(q // 2) * 256 + 256]
                        act.wait_ge(half_used, used(f"in{s}", tau // 2, 1))
                        act.activation(dst[:, 0:2, :], bank[(tau - 1) % 4][:].rearrange("p (t n) -> p t n", t=2),
                                       ACT.Copy).then_inc(proj_out, 1)
                        act.activation(dst[:, 2, :], bank[tau % 4][:, 0:256], ACT.Copy).then_inc(proj_out, 1)
                        halves_ahead[0]()
                        halves_ahead[1]()
                        return
                    halves_ahead[tau % 2]()
                    dst = {0: QF, 1: FF, 2: FB, 4: G, 5: BQ, 6: BK}[part][:, q, :]
                    act.wait_ge(half_used, used(f"in{s}", tau // 2, tau % 2))
                    act.activation(dst, cols3(bank[tau % 4]), ACT.Copy).then_inc(proj_out, 1)

                for tau in range(12):
                    proj(tau)
                act.wait_ge(ctx_turned, 1)
                act.activation(CKT.rearrange("p a b -> p (a b)"), bank[6][:], ACT.Copy).then_inc(ctx_ready, 1)
                act.wait_ge(proj_out, 12)
                act.dma_start(cache_v_new[0, 0].rearrange("h t d -> t h d"),
                              BV[:, 0, :].rearrange("p (h d) -> p h d", h=HEADS_B)).then_inc(kv_stored, 16)
                for step in range(24 + 3):
                    u = step
                    if u < 24:
                        act.wait_ge(s_max, 2 * u + 2)
                        if u >= 4:
                            act.wait_ge(p_turned, u - 3)
                        n = P if u % 3 == 0 else NT
                        act.activation(TT[:, u % 4, 0:n], bank[4 + u % 2][:, 0:n], ACT.Exp,
                                       bias=SMALL[:, 0, u % 4:u % 4 + 1], scale=DH ** -0.5,
                                       accum_out=SMALL[:, 1, u % 4:u % 4 + 1]).then_inc(s_exp, 1)
                    u = step - 2
                    if 0 <= u < 24:
                        n = P if u % 3 == 0 else NT
                        act.wait_ge(p_turned, u + 1)
                        if u >= 2:
                            act.wait_ge(pv_done, u - 1)
                        act.activation(SQ[:, u % 2, 0:n], bank[6][:, 0:n], ACT.Copy).then_inc(p_copied, 1)
                    u = step - 3
                    if 0 <= u < 24 and u % 6 == 5:
                        act.wait_ge(pv_done, u + 1)
                        act.activation(BQ[:, u // 6, :], cols3(bank[7]), ACT.Copy).then_inc(ob_done, 1)
                    if step < 20:
                        proj(12 + step)
                g0 = first_group("modC")
                mod_rows_out(g0)
                mod_cols_out(g0)
                act.wait_ge(kout_turned, 1)
                act.activation(KOUT, bank[6][:], ACT.Copy).then_inc(kout_ready, 1)
                act.wait_ge(kout_ready, 1)
                act.dma_start(cache_k_new[0, 0].rearrange("h t d -> t h d"),
                              KOUT.rearrange("p (h d) -> p h d", h=HEADS_B)).then_inc(kv_stored, 16)
                mod_rows_out(g0 + 1)
                act.wait_ge(proj_out, 32)
                for w, (z, k) in enumerate(((FF, KFW), (FB, KBW))):
                    act.activation(k, z, ACT.Sigmoid, scale=-1.0).then_inc(sig_done, 1)
                    act.wait_ge(sig_done, 2 * w + 1)
                    act.activation(z, z, ACT.Sigmoid).then_inc(sig_done, 1)
                mod_cols_out(g0 + 1)
                mod_rows_out(g0 + 2)
                act.activation(OUTF[:, 0:4, :], G, ACT.Sigmoid).then_inc(sig_done, 1)
                for ht in range(4):
                    act.activation(HH[:, 4 + ht, :], BQ[:, ht, :], ACT.Copy).then_inc(cat_hi, 1)
                mod_cols_out(g0 + 2)
                for g in range(g0 + 3, g0 + 6):
                    mod_rows_out(g)
                    mod_cols_out(g)
                act.wait_ge(kv_stored, 32)
                for h in range(HEADS_A):
                    act.wait_ge(k_turned, h + 1)
                    if h >= 2:
                        act.wait_ge(st_mm, h - 1)
                    act.activation(KTOK[:, h % 2].rearrange("p j t -> p (j t)"), bank[5][:],
                                   ACT.Copy).then_inc(k_copied, 1)
                    split_act(act, f"out{s}", h // 2, 8)[h % 2]()
                def head_root(h):
                    act.wait_ge(o_stat, h + 1)
                    if h >= 1:
                        act.wait_ge(o_step, 3 * (h - 1) + 1)
                    act.activation(ROOT[:], cols3(bank[h]), ACT.Sqrt, bias=EPSC[:, 0:1],
                                   scale=1.0 / P).then_inc(o_root, 1)

                for h in range(HEADS_A):
                    act.wait_ge(st_ready, 4 * h + 4)
                    if h == 0:
                        act.wait_ge(st_ready, 4 * HEADS_A)
                        for w in range(2):
                            act.dma_start(state_new[0, 0, w].rearrange("h k v -> k h v"),
                                          (KFW, KBW)[w][:, :, 0:P]).then_inc(state_stored, 16)
                    act.wait_ge(o_mm, h + 1)
                    if h >= 2:
                        act.wait_ge(o_stat, h - 1)
                    act.activation(SQ[:, h % 2, :], cols3(bank[h]), ACT.Square).then_inc(o_sq, 1)
                    act.activation(FF[:, h, :], cols3(bank[h]), ACT.Copy).then_inc(o_copied, 1)
                    if h == 1:
                        head_root(0)
                for h in range(1, HEADS_A + 1):
                    if h < HEADS_A:
                        head_root(h)
                    if h >= 1:
                        act.wait_ge(o_step, 3 * h)
                        act.activation(HH[:, h - 1, :], FF[:, h - 1, :], ACT.Copy).then_inc(cat_hi, 1)
                act.wait_ge(state_stored, 32)
                for n in range(4):
                    for b in range(2):
                        ahead(act, split_act, s, "out", n)[b]()
                        out_tile(s, OUTM, f"out{s}", n, b, 2 * n + b)

            def odd(s):
                for tau in range(24):
                    if tau % 2 == 0:
                        for half in ahead(act, split_act, s, "in", tau // 2):
                            half()
                    d = tau % 8
                    if tau < 16:
                        act.wait_ge(half_used, used(f"in{s}", tau // 2, tau % 2))
                        dst = (CB if tau < 8 else CG)[:, d, :]
                        for g, (t0, t1) in enumerate(GROUPS):
                            a = act.activation(dst[:, t0 + 1 + g:t1 + 1 + g], bank[tau % 4][:, t0:t1], ACT.Copy)
                        a.then_inc(proj_out, 1)
                for d in range(KD):
                    if d == 6:
                        mod_rows_out(first_group(MIDDLE[s]))
                        mod_cols_out(first_group(MIDDLE[s]))
                    act.wait_ge(conv_done, d + 1)
                    if d == 0:
                        act.wait_ge(half_used, used(f"in{s}", 11, 1))
                    for g, (t0, t1) in enumerate(GROUPS):
                        a = act.activation(HH[:, d, t0:t1], CG[:, d, t0 + 1 + g:t1 + 1 + g], ACT.Copy)
                    a.then_inc(cat_hi, 1)
                for n in range(4):
                    for b in range(2):
                        ahead(act, split_act, s, "out", n)[b]()
                        out_tile(s, OUTC, f"out{s}", n, b, 2 * n + b)

            mod_rows_out(0)
            mod_cols_out(0)
            mod_rows_out(1)
            mod_cols_out(1)
            pre(0)
            for s in range(upto):
                {"ffn": ffn, "even": even, "odd": odd}[SUBLAYERS[s][0]](s)
                post(s)
                if s < upto - 1:
                    pre(s + 1)
            for n in range(2 * TOKS):
                b, t = divmod(n, TOKS)
                act.wait_ge(y_copied, n + 1)
                half = slice(b * 512, (b + 1) * 512)
                act.dma_start([y_prompt[0][:, half], y_sample[0, 0:P, half], y_sample[0, P:2 * P, half]][t],
                              XS[:, t, half]).then_inc(y_stored, 16)
            act.wait_ge(y_stored, 32 * TOKS)

        @block.vector
        def _(dve):
            dve.sem_inc(gated, 2)
            dve.sem_inc(act_ready, 2)
            dve.wait_ge(tp_done, 1)
            dve.tensor_copy(PAR[:, 0:PAR_ROWS], bank[0][:, 0:PAR_ROWS]).then_inc(par_ready, 1)
            lb_in = PAR[:, PAR_LB:PAR_LB + 8]
            dve.wait_ge(par_ready, 1)
            dve.tensor_tensor(LBT[:, 1, :], lb_in, lb_in, ALU.subtract).then_inc(lb_step, 1)
            dve.wait_ge(lb_step, 2)
            dve.reciprocal(LBT[:, 1, :], LBT[:, 0, :]).then_inc(lb_step, 1)
            dve.wait_ge(lb_step, 3)
            dve.tensor_tensor(LBT[:, 2, :], LBT[:, 0, :], LBT[:, 1, :], ALU.mult).then_inc(lb_step, 1)
            dve.wait_ge(lb_step, 4)
            dve.tensor_tensor(LBT[:, 3, :], LBT[:, 2, :], LBT[:, 2, :], ALU.subtract).then_inc(lb_step, 1)
            dve.wait_ge(lb_step, 5)
            dve.tensor_scalar(LBT[:, 2, :], LBT[:, 3, :], 0.0, LB_MAX, ALU.max, ALU.min).then_inc(lb_step, 1)
            dve.wait_ge(lb_step, 6)
            dve.tensor_scalar(LBT[:, 3, :], LBT[:, 2, :], -1.0, 1.0, ALU.mult, ALU.add).then_inc(lb_step, 1)
            for d in range(KD):
                dve.wait_ge(tp_done, 2 + d)
                x = dve.tensor_copy(X[:, d, :], cols3(bank[1 + d % 4]))
                if d % 2:
                    x.then_inc(x_ready, 1)
                else:
                    x.then_inc(delta, 1)

            def coefficients(g):
                m = MOD[:, 8 * g:8 * g + 8, :]
                dve.wait_ge(mod_cols, g + 1)
                dve.tensor_tensor(m, m, PAR[:, 8 * g:8 * g + 8].rearrange("p (t g) -> p t g", g=1)
                                  .broadcast_to([P, 8, 2]), ALU.add).then_inc(coef_step, 1)
                dve.wait_ge(coef_step, g + 1)
                b, part = divmod(g, 3)
                if part == 0:
                    dve.sem_inc(coef_ready, 1)
                    return
                norm = (PAR_PRE if part == 1 else PAR_POST) + 8 * b
                gain = PAR[:, norm:norm + 8].rearrange("p (t g) -> p t g", g=1).broadcast_to([P, 8, 2])
                if part == 1:
                    c_ = dve.scalar_tensor_tensor(CA[:, b], m, 1.0, gain, ALU.add, ALU.mult)
                else:
                    c_ = dve.scalar_tensor_tensor(CC[:, b], m, HALF[b], gain, ALU.mult, ALU.mult)
                c_.then_inc(coef_ready, 1)

            def rstd(n):
                dve.wait_ge(root_done, n)
                dve.reciprocal(RSTD[:], ROOT[:]).then_inc(rstd_done, 1)
                dve.wait_ge(rstd_done, n)

            def pre(s):
                rstd(2 * s + 1)
                groups = between(s)
                now = [g for g in groups if g <= 3 * s + 1]
                for g in now:
                    coefficients(g)
                dve.wait_ge(coef_ready, 3 * s + 2)

                def scaled(d):
                    if d >= 2:
                        dve.wait_ge(h_hi, 8 * s + d - 1)
                        dve.wait_ge(h_full, 8 * s + d - 1)
                    dve.tensor_tensor(TT[:, d % 2, :], X[:, d, :], RSTD[:], ALU.mult).then_inc(h_scaled, 1)

                scaled(0)
                for d in range(KD):
                    if d + 1 < KD:
                        scaled(d + 1)
                    dve.wait_ge(h_scaled, 8 * s + d + 1)
                    if d >= 2:
                        dve.wait_ge(h_ready, 8 * s + d - 1)
                    for g, (t0, t1) in enumerate(GROUPS):
                        x = dve.tensor_scalar(TT[:, 2 + d % 2, t0:t1], TT[:, d % 2, t0:t1], CA[:, s, d, g:g + 1],
                                              MOD[:, 24 * s + d, g:g + 1], ALU.mult, ALU.add)
                    x.then_inc(h_full, 1)
                    dve.wait_ge(h_full, 8 * s + d + 1)
                    dve.wait_ge(h_hi, 8 * s + d + 1)
                    dve.tensor_tensor(HL[:, d, :], TT[:, 2 + d % 2, :], HH[:, d, :].bitcast(F32),
                                      ALU.subtract).then_inc(h_ready, 1)
                for g in groups[len(now):]:
                    coefficients(g)
                dve.wait_ge(half_ready, 2 * stages[f"in{s}"]["m"] + 4)

            def add_square(s, d):
                dve.wait_ge(out_sq, 8 * s + d + 1)
                if d == 0:
                    dve.tensor_copy(ACC[:], SQ[:, 0, :]).then_inc(sq_added, 1)
                else:
                    dve.wait_ge(sq_added, 8 * s + d)
                    dve.tensor_tensor(ACC[:], ACC[:], SQ[:, d % 2, :], ALU.add).then_inc(sq_added, 1)

            def post(s, OUT):
                rstd(2 * s + 2)
                dve.wait_ge(out_done, 4 + 8 * (s + 1))
                for pp in range(4):
                    if pp >= 2:
                        dve.wait_ge(out_scaled, 2 * s + pp - 1)
                        dve.tensor_tensor(X[:, 2 * pp:2 * pp + 2, :], X[:, 2 * pp:2 * pp + 2, :],
                                          OUT[:, 2 * pp:2 * pp + 2, :], ALU.add).then_inc(x_ready, 1)
                        continue
                    if pp:
                        dve.wait_ge(x_ready, 4 * s + 4 + pp)
                    dve.tensor_tensor(TT[:, 0:2, :], OUT[:, 2 * pp:2 * pp + 2, :],
                                      RSTD[:].rearrange("p (a n) -> p a n", a=1).broadcast_to([P, 2, NT]),
                                      ALU.mult).then_inc(delta, 1)
                    dve.wait_ge(delta, 4 + 2 * s + pp + 1)
                    dve.tensor_tensor(X[:, 2 * pp:2 * pp + 2, :], X[:, 2 * pp:2 * pp + 2, :], TT[:, 0:2, :],
                                      ALU.add).then_inc(x_ready, 1)

            def ffn(s):
                f, st = SUBLAYERS[s][1], f"in{s}"

                def pair(i, j):
                    nxt = [split_dve(dve, st, j + 2 + q, 8, i) for q in range(2)] if j < 20 else \
                        [split_dve(dve, f"out{s}", q, 8) for q in range(2)]
                    base = 22 * f + j
                    nxt[0][0]()
                    nxt[0][1]()
                    for b in range(2):
                        nxt[1][b]()
                        dve.wait_ge(silu_done, i * 6 + (2 + base + b + 1))
                        dve.wait_ge(half_used, i * 12 + used(st, j + 1, b))
                        dve.wait_ge(act_ready, i * 6 + (base + b + 1))
                        dve.tensor_tensor(TT[:, 2 + b, :], TT[:, b, :], cols3(bank[2 + b]),
                                          ALU.mult).then_inc(gated, 1)
                    for b in range(2):
                        dve.wait_ge(act_hi, i * 6 + (base + b + 1))
                        at = bass.ds(i * 6 + (j + b), 1)
                        dve.tensor_tensor(AL[:, at, :], TT[:, 2 + b:3 + b, :], AH[:, at, :].bitcast(F32),
                                          ALU.subtract).then_inc(act_ready, 1)

                ffn_pairs(dve, pair)
                if s < 5:
                    coefficients(first_group(MIDDLE[s]))
                for n in range(12):
                    for half in ahead(dve, split_dve, s, "out", n):
                        half()
                    if n % 3 == 2:
                        for b in range(2):
                            add_square(s, 2 * (n // 3) + b)

            def even(s):
                def proj(tau):
                    halves_ahead = ahead(dve, split_dve, s, "in", tau // 2)
                    if AB_ORDER[tau // 2] // 2 not in (3, 7):
                        halves_ahead[tau % 2]()
                    elif tau % 2:
                        halves_ahead[0]()
                        halves_ahead[1]()

                for tau in range(12):
                    proj(tau)
                for step in range(24 + 3):
                    u = step
                    if u < 24:
                        top = SMALL[:, 0, u % 4:u % 4 + 1]
                        dve.wait_ge(s_mm, u + 1)
                        dve.tensor_reduce(top, bank[4 + u % 2][:, 0:P if u % 3 == 0 else NT], AX.X,
                                          ALU.max, negate=True).then_inc(s_max, 1)
                        dve.wait_ge(s_max, 2 * u + 1)
                        dve.tensor_scalar(top, top, DH ** -0.5, None, ALU.mult).then_inc(s_max, 1)
                    u = step - 1
                    if 0 <= u < 24:
                        n = P if u % 3 == 0 else NT
                        dve.wait_ge(s_exp, u + 1)
                        dve.reciprocal(SMALL[:, 2, u % 4:u % 4 + 1], SMALL[:, 1, u % 4:u % 4 + 1]).then_inc(p_inv, 1)
                        dve.wait_ge(p_inv, u + 1)
                        dve.tensor_scalar(TT[:, u % 4, 0:n], TT[:, u % 4, 0:n], SMALL[:, 2, u % 4:u % 4 + 1], None,
                                          ALU.mult).then_inc(p_ready, 1)
                    if step < 20:
                        proj(12 + step)
                n = [0]

                def tick(x):
                    x.then_inc(prep, 1)
                    n[0] += 1

                def gate(t, w, k=False):
                    for h in range(HEADS_A):
                        lb, one_less = LBT[:, 2, 4 * w + h:4 * w + h + 1], LBT[:, 3, 4 * w + h:4 * w + h + 1]
                        if k:
                            tick(dve.tensor_scalar(t[:, h, :], t[:, h, :], one_less, None, ALU.mult))
                        else:
                            tick(dve.tensor_scalar(t[:, h, :], t[:, h, :], one_less, lb, ALU.mult, ALU.add))

                dve.wait_ge(sig_done, 2)
                gate(FF, 0)
                dve.wait_ge(sig_done, 3)
                gate(KBW, 1, k=True)
                dve.wait_ge(sig_done, 4)
                gate(FB, 1)
                dve.wait_ge(kout_turned, 1)
                dve.wait_ge(k_scaled, HEADS_A)
                dve.wait_ge(prep, 12)
                tick(dve.tensor_tensor(KS, KFW.rearrange("p h n -> p (h n)").rearrange("p (u t) -> p u t", u=UNITS),
                                       KBW.rearrange("p h n -> p (h n)").rearrange("p (u t) -> p u t", u=UNITS),
                                       ALU.add))
                tick(dve.tensor_scalar(FF, FF, 1e-30, None, ALU.max))
                tick(dve.tensor_scalar(FB, FB, 1e-30, None, ALU.max))
                dve.wait_ge(prep, 15)
                tick(dve.tensor_tensor(QB, QF, FB, ALU.mult))
                dve.wait_ge(kv_stored, 32)
                for cc in range(3):
                    dve.wait_ge(diag_mm, cc + 1)
                    dve.tensor_copy(ATT[:, 4 * cc:4 * cc + 4, :],
                                    bank[cc][:].rearrange("p (u t) -> p u t", u=4)).then_inc(diag_out, 1)
                tick(dve.tensor_tensor(QF, QF, FF, ALU.mult))

                def silu_g():
                    dve.wait_ge(sig_done, 5)
                    dve.tensor_tensor(G, G, OUTF[:, 0:4, :], ALU.mult).then_inc(g_ready, 1)

                def cat_lo(ht):
                    dve.wait_ge(cat_hi, ht + 1)
                    dve.tensor_tensor(HL[:, 4 + ht, :], BQ[:, ht, :], HH[:, 4 + ht, :].bitcast(F32),
                                      ALU.subtract).then_inc(cat_ready, 1)

                meanwhile = [silu_g] + [lambda ht=ht: cat_lo(ht) for ht in range(4)]
                assert n[0] == PREP, n
                for lv in range(LEVELS):
                    b = 1 << lv
                    for w in range(2):
                        q, f = (QF, QB)[w], (FF, FB)[w]
                        dve.wait_ge(lvl_mm, 2 * lv + w + 1)
                        if lv == 0:
                            dve.wait_ge(diag_out, 3)
                        out = ATT.rearrange("p u (m w i) -> p u m w i", w=2, i=b)[:, :, :, 1 - w, :]
                        for half in range(2):
                            if lv + w:
                                dve.wait_ge(lvl_out, 4 * lv + 2 * w + half - 1)
                            mask = LMASK[:, 2 * lv + w, :].rearrange("p (u m i) -> p u m i", u=1, i=b)
                            dve.copy_predicated(out[:, 6 * half:6 * half + 6],
                                                mask.broadcast_to([P, 6, P // (2 * b), b]),
                                                bank[3 + 2 * w + half][:, 0:6 * 64].rearrange(
                                                    "p (u m i) -> p u m i", u=6, i=b)).then_inc(lvl_out, 1)
                        if lv == 0:
                            dve.wait_ge(prep, PREP)
                        else:
                            dve.wait_ge(lvl_t, 2 * (lv - 1) + w + 1)
                        qh = halves(q, b)[:, :, 1 - w, :]
                        dve.tensor_tensor(qh, qh, total(f, b, w), ALU.mult).then_inc(lvl_q, 1)
                        if 2 * lv + w < len(meanwhile):
                            meanwhile[2 * lv + w]()
                        dve.wait_ge(lvl_k, 2 * lv + w + 1)
                        dve.wait_ge(lvl_q, 2 * lv + w + 1)
                        tl, tr = halves(f, b)[:, :, 0, 0:1], halves(f, b)[:, :, 1, 0:1]
                        dve.tensor_tensor(tl, tl, tr, ALU.mult).then_inc(lvl_t, 1)
                for g in range(first_group("modC"), first_group("modD")):
                    coefficients(g)
                dve.wait_ge(state_landed, 16)
                dve.wait_ge(lvl_t, 2 * LEVELS)
                for h in range(HEADS_A):
                    dve.wait_ge(st_mm, h + 1)
                    B = bank[3 + h % 2]
                    for w in range(2):
                        k, f = (KFW, KBW)[w], (FF, FB)[w]
                        unit = 1 + w
                        dve.tensor_copy(k[:, h, 0:P], B[:, 256 * w:256 * w + P]).then_inc(st_ready, 1)
                        dve.scalar_tensor_tensor(k[:, h, P:2 * P], ST[:, 4 * w + h, :], f[:, h, unit * P:unit * P + 1],
                                                 B[:, 256 * w + P:256 * w + 256], ALU.mult, ALU.add) \
                            .then_inc(st_ready, 1)
                def head_lo(h):
                    dve.wait_ge(cat_hi, 4 + h + 1)
                    dve.tensor_tensor(HL[:, h, :], FF[:, h, :], HH[:, h, :].bitcast(F32),
                                      ALU.subtract).then_inc(cat_ready, 1)

                dve.wait_ge(g_ready, 1)
                for h in range(HEADS_A):
                    dve.wait_ge(o_root, h + 1)
                    dve.reciprocal(RSTD[:], ROOT[:]).then_inc(o_step, 1)
                    if h:
                        head_lo(h - 1)
                    dve.wait_ge(o_step, 3 * h + 1)
                    dve.tensor_tensor(FF[:, h, :], FF[:, h, :], RSTD[:], ALU.mult).then_inc(o_step, 1)
                    dve.wait_ge(o_step, 3 * h + 2)
                    dve.scalar_tensor_tensor(FF[:, h, :], FF[:, h, :], PAR[:, PAR_GN:PAR_GN + 1], G[:, h, :],
                                             ALU.mult, ALU.mult).then_inc(o_step, 1)
                head_lo(HEADS_A - 1)
                dve.wait_ge(half_ready, 2 * stages[f"out{s}"]["m"] + 4)
                for n_ in range(4):
                    for half in ahead(dve, split_dve, s, "out", n_):
                        half()
                    for b in range(2):
                        add_square(s, 2 * n_ + b)

            def odd(s):
                for t in (CB, CG, U):
                    for at in (0, SEQ + 1, PADDED - 1):
                        x = dve.memset(t[:, :, at:at + 1], 0.0)
                x.then_inc(pads_set, 1)
                dve.wait_ge(pads_set, 1)
                def conv_lo(d):
                    dve.wait_ge(cat_hi, 8 + d + 1)
                    dve.wait_ge(conv_done, d + 1)
                    for g, (t0, t1) in enumerate(GROUPS):
                        x = dve.tensor_tensor(HL[:, d, t0:t1], CG[:, d, t0 + 1 + g:t1 + 1 + g],
                                              HH[:, d, t0:t1].bitcast(F32), ALU.subtract)
                    x.then_inc(cat_ready, 1)

                for tau in range(24):
                    if tau % 2 == 0:
                        for half in ahead(dve, split_dve, s, "in", tau // 2):
                            half()
                    if tau < 16:
                        continue
                    d = tau - 16
                    if d == 6:
                        conv_lo(0)
                        conv_lo(1)
                    if d == 7:
                        conv_lo(2)
                        conv_lo(3)
                        conv_lo(4)
                    dve.wait_ge(half_used, used(f"in{s}", tau // 2, tau % 2))
                    dve.wait_ge(proj_out, 32 + 8 + d + 1)
                    for g, (t0, t1) in enumerate(GROUPS):
                        x = dve.tensor_tensor(U[:, d % 2, t0 + 1 + g:t1 + 1 + g], bank[tau % 4][:, t0:t1],
                                              CG[:, d, t0 + 1 + g:t1 + 1 + g], ALU.mult)
                    x.then_inc(conv_step, 1)
                    dve.wait_ge(conv_step, 4 * d + 1)
                    if d:
                        dve.wait_ge(conv_done, d)
                    n = PADDED - 2
                    taps = [PAR[:, PAR_CONV + 8 * w + d:PAR_CONV + 8 * w + d + 1] for w in range(3)]
                    y = Y[:, 0:n]
                    dve.tensor_scalar(y, U[:, d % 2, 1:1 + n], taps[1], None, ALU.mult).then_inc(conv_step, 1)
                    for q, w in enumerate((0, 2)):
                        dve.wait_ge(conv_step, 4 * d + 2 + q)
                        dve.scalar_tensor_tensor(y, U[:, d % 2, w:w + n], taps[w], y, ALU.mult,
                                                 ALU.add).then_inc(conv_step, 1)
                    dve.wait_ge(conv_step, 4 * d + 4)
                    dve.wait_ge(proj_out, 32 + d + 1)
                    dve.tensor_tensor(CG[:, d, 1:1 + n], y, CB[:, d, 1:1 + n], ALU.mult).then_inc(conv_done, 1)
                for d in range(5, KD):
                    conv_lo(d)
                coefficients(first_group(MIDDLE[s]))
                for n in range(4):
                    for half in ahead(dve, split_dve, s, "out", n):
                        half()
                    for b in range(2):
                        add_square(s, 2 * n + b)

            coefficients(0)
            coefficients(1)
            pre(0)
            for s in range(upto):
                kind = SUBLAYERS[s][0]
                {"ffn": ffn, "even": even, "odd": odd}[kind](s)
                post(s, {"ffn": OUTF, "even": OUTM, "odd": OUTC}[kind])
                if s < upto - 1:
                    pre(s + 1)
            for n in range(2 * TOKS):
                b, t = divmod(n, TOKS)
                dve.wait_ge(tp_done, 9 + n + 1)
                dve.tensor_copy(XS[:, t, b * 512:(b + 1) * 512], bank[n % 4 + 4][:]).then_inc(y_copied, 1)

        @block.tensor
        def _(pe):
            pe.sem_inc(half_used, 4)
            pe.wait_ge(setup_landed, 16 * 14)
            for t in range(3):
                n = min(P, PAR_ROWS - t * P)
                mm = pe.transpose(bank[0][:, t * P:t * P + n], PS[0:n, t, :], IDENT[0:n, 0:n])
            mm.then_inc(tp_done, 1)
            pe.wait_ge(x_landed, 48)
            for d in range(KD):
                if d >= 4:
                    pe.wait_ge(delta, (d - 4) // 2 + 1) if d % 2 == 0 else pe.wait_ge(x_ready, (d - 4) // 2 + 1)
                for t in range(TOKS):
                    mm = pe.transpose(bank[1 + d % 4][:, t * P:(t + 1) * P], XS[:, t, d * P:(d + 1) * P], IDENT[:])
                mm.then_inc(tp_done, 1)

            def mod_slot(st, n):
                k = 4 * first_group(st) + n
                g, q = divmod(k, 4)
                p, uses = ring_at(st, n)
                if q == 0 and g >= 2:
                    pe.wait_ge(mod_cols, g - 1)
                pe.wait_ge(raw_landed[p], 16 * (uses + 1))
                for kk in range(KD):
                    mm = pe.matmul(bank[MOD_BANK[g]][32 * q:32 * q + 32, 0:256], COND[:, kk, :],
                                   RAW[:, p, kk, :], start=(kk == 0), stop=(kk == KD - 1))
                mm.then_inc(mod_used, 1)

            def mod_turn(g):
                pick = IDENT[:].rearrange("p (q r) -> p q r", r=32)[:, :, 0:2]
                B = bank[MOD_BANK[g]]
                pe.wait_ge(mod_rows, g + 1)
                for h in range(2):
                    mm = pe.matmul(B[:, 8 * h:8 * h + 8].rearrange("p (q g) -> p q g", g=2),
                                   ROWS[:, h * P:(h + 1) * P], pick, start=True, stop=True)
                mm.then_inc(mod_turned, 1)

            def mod_stage(st):
                g0 = first_group(st)
                for n in range(stages[st]["n"]):
                    mod_slot(st, n)
                    if n >= 4 and n % 4 == 2:
                        mod_turn(g0 + n // 4 - 1)
                mod_turn(g0 + stages[st]["n"] // 4 - 1)

            def pre_stats(s):
                pe.wait_ge(const_set, 1)
                for pp in range(4):
                    pe.wait_ge(xsq_done, 4 * s + pp + 1)
                    for b in range(2):
                        src = SQ[:, b, :] if pp % 2 == 0 else TT[:, 2 + b, :]
                        mm = pe.matmul(cols3(bank[1]), ONES[:], src, start=(pp + b == 0), stop=(pp == 3 and b == 1))
                    mm.then_inc(stat_done, 1)

            def first_four(s):
                for _ in pe_four(pe, f"in{s}", [cols3(bank[b]) for b in range(4)], range(KD),
                                 lambda kk: pe.wait_ge(h_ready, 8 * s + kk + 1)):
                    pass

            def post_stats(s):
                pe.wait_ge(sq_added, 8 * s + 8)
                pe.matmul(cols3(bank[0]), ONES[:], ACC[:], start=True, stop=True).then_inc(stat_done, 1)

            def ffn(s):
                f, st = SUBLAYERS[s][1], f"in{s}"

                def pair(i, j):
                    base = 22 * f + j
                    if j == 0:
                        pe.wait_ge(silu_done, base + 2)
                        pe.wait_ge(gated, base + 2)
                        first_four(s)
                        return
                    for b in range(2):
                        pe.wait_ge(silu_done, i * 6 + (base + b + 1))
                        pe_half(pe, st, 2 * j + b, hh, hl, 8, cols3(bank[b]), True, True, i)
                    for b in range(2):
                        pe.wait_ge(gated, i * 6 + (base + b + 1))
                        pe_half(pe, st, 2 * j + 2 + b, hh, hl, 8, cols3(bank[2 + b]), True, True, i)

                ffn_pairs(pe, pair)
                if s < 5:
                    mod_stage(MIDDLE[s])
                pe.wait_ge(mod_cols, first_group(BETWEEN[s]) if s < 5 else 18)
                st = f"out{s}"

                def quarter_pair(i):
                    for j in range(6):
                        r = j % 3
                        for b in range(2):
                            t = 2 * (j // 3) + b
                            if r == 0:
                                pe.wait_ge(out_done, i * 4 + (8 * s + t + 1))
                            if b == 0:
                                pe.wait_ge(act_ready, 2 + 22 * f + min(8 * r + 8, KF))
                            pe_half(pe, st, 2 * j + b, lambda kk: AH[:, 8 * r + kk, :],
                                    lambda kk: AL[:, 8 * r + kk, :], out_nk(st, j), cols3(bank[4 + t]),
                                    r == 0, r == 2, i)

                with pe.Fori(0, 2) as i:
                    quarter_pair(i)

            def out_four(s, order, ready):
                pe.wait_ge(mod_cols, first_group(BETWEEN[s]))
                pe.wait_ge(out_done, 8 * s + 4)
                return pe_four(pe, f"out{s}", [cols3(bank[4 + b]) for b in range(4)], order, ready)

            def out_small(s):
                for n in range(2, 4):
                    for b in range(2):
                        d = 2 * n + b
                        pe.wait_ge(out_done, 8 * s + d + 1)
                        pe_half(pe, f"out{s}", d, hh, hl, 8, cols3(bank[4 + d % 4]), True, True)

            def even(s):
                def proj(tau):
                    if tau >= 4:
                        pe.wait_ge(proj_out, tau - 3)
                    part = AB_ORDER[tau // 2] // 2
                    if part not in (3, 7):
                        pe_half(pe, f"in{s}", tau, hh, hl, 8, cols3(bank[tau % 4]), True, True)
                        return
                    j = tau // 2
                    H = 2 * (stages[f"in{s}"]["m"] + j)
                    k = H % 4
                    pe.wait_ge(half_ready, H + 2)
                    for t in ((0, 1), (2,))[tau % 2]:
                        out = bank[tau % 4][:, (t % 2) * 256:(t % 2) * 256 + 256].rearrange("p (b n) -> p b n", b=2)
                        tok = slice(t * P, (t + 1) * P)
                        for kk in range(KD):
                            pe.matmul(out, HH[:, kk, tok], WH[:, k:k + 2, kk, :], start=(kk == 0), stop=False)
                            pe.matmul(out, HL[:, kk, tok], WH[:, k:k + 2, kk, :], start=False, stop=False)
                            mm = pe.matmul(out, HH[:, kk, tok], WL[:, k:k + 2, kk, :], start=False,
                                           stop=(kk == KD - 1))
                    if tau % 2:
                        mm.then_inc(half_used, 2)

                first_four(s)
                for tau in range(4, 12):
                    proj(tau)
                pe.wait_ge(ctx_landed, 32)
                for ht in range(4):
                    mm = pe.transpose(bank[6][:, ht * P:(ht + 1) * P], CKR[:, ht * P:(ht + 1) * P], IDENT[:])
                mm.then_inc(ctx_turned, 1)
                pe.wait_ge(proj_out, 12)
                pe.wait_ge(ctx_ready, 1)
                filled = [0]
                g0 = first_group("modC")

                def fill(count):
                    for _ in range(count):
                        n = filled[0]
                        filled[0] += 1
                        mod_slot("modC", n)
                        if n % 4 == 2 and n // 4 not in (0, 3):
                            mod_turn(g0 + n // 4 - 1)

                for step in range(24 + 3):
                    u = step
                    if u < 24:
                        h, i = divmod(u, 3)
                        ht, pb = h // 2, DH * (h % 2)
                        S = bank[4 + u % 2]
                        if u >= 2:
                            pe.wait_ge(s_exp, u - 1)
                        q = BQ[pb:pb + DH, ht, i * P:(i + 1) * P]
                        if i == 0:
                            mm = pe.matmul(S[:, 0:P], q, BK[pb:pb + DH, ht, 0:P], start=True, stop=True)
                        else:
                            if i == 1:
                                pe.wait_ge(bias_ready, h + 1)
                            x0 = (2 - 2 * (i - 1)) * GRID_W
                            pe.matmul(S[:, 0:DEC_SEQ], q, BK[pb:pb + DH, ht, SEQ:NT], start=True, stop=False)
                            pe.matmul(S[:, 0:DEC_SEQ], FLIP[:], BIAS.rearrange("p a b -> p (a b)")
                                      [:, x0:x0 + DEC_SEQ], start=False, stop=True)
                            mm = pe.matmul(S[:, DEC_SEQ:NT], q, CKT[pb:pb + DH, ht, :], start=True, stop=True)
                        mm.then_inc(s_mm, 1)
                    u = step - 2
                    if 0 <= u < 24:
                        pe.wait_ge(p_ready, u + 1)
                        if u >= 1:
                            pe.wait_ge(p_copied, u)
                        for t in range(1 if u % 3 == 0 else 3):
                            mm = pe.transpose(bank[6][:, t * P:(t + 1) * P], TT[:, u % 4, t * P:(t + 1) * P], IDENT[:])
                        mm.then_inc(p_turned, 1)
                    u = step - 3
                    if 0 <= u < 24:
                        h, i = divmod(u, 3)
                        pb = DH * (h % 2)
                        out = bank[7][pb:pb + DH, i * P:(i + 1) * P]
                        pe.wait_ge(p_copied, u + 1)
                        if u % 6 == 0 and u:
                            pe.wait_ge(ob_done, u // 6)
                        vals = [BV[:, 0, h * DH:(h + 1) * DH]] if i == 0 else \
                            [BV[:, 1, h * DH:(h + 1) * DH], BV[:, 2, h * DH:(h + 1) * DH], CV[:, h, :]]
                        for t, v in enumerate(vals):
                            mm = pe.matmul(out, v, SQ[:, u % 2, t * P:(t + 1) * P], start=(t == 0),
                                           stop=(t == len(vals) - 1))
                        mm.then_inc(pv_done, 1)
                    if step < 20:
                        proj(12 + step)
                    else:
                        pe.wait_ge(proj_out, 32)
                        fill(1)
                for ht in range(4):
                    mm = pe.transpose(bank[6][:, ht * P:(ht + 1) * P], BK[:, ht, 0:P], IDENT[:])
                mm.then_inc(kout_turned, 1)

                def unit(t, u):
                    return t[:, u // TOKS, (u % TOKS) * P:(u % TOKS + 1) * P]

                fill(5)
                pe.wait_ge(mod_cols, g0 + 2)
                pe.wait_ge(prep, 13)
                for u in range(UNITS):
                    mm = pe.matmul(bank[u // 4][:, (u % 4) * P:(u % 4 + 1) * P], KS[:, u, :], unit(QF, u),
                                   start=True, stop=True)
                    if u % 4 == 3:
                        mm.then_inc(diag_mm, 1)
                mod_turn(g0 + 2)
                pe.wait_ge(mod_cols, g0 + 3)
                for lv in range(LEVELS):
                    b = 1 << lv
                    for w in range(2):
                        q, k = (QF, QB)[w], (KFW, KBW)[w]
                        if lv == 0:
                            pe.wait_ge(prep, PREP)
                        else:
                            pe.wait_ge(lvl_q, 2 * (lv - 1) + w + 1)
                            pe.wait_ge(lvl_k, 2 * (lv - 1) + w + 1)
                            pe.wait_ge(lvl_out, 4 * (lv - 1) + 2 * w + 2)
                        for u in range(UNITS):
                            rhs = unit(q, u).rearrange("p (m w i) -> p m w i", w=2, i=b)[:, :, 1 - w, :]
                            out = bank[3 + 2 * w + u // 6][:, (u % 6) * 64:(u % 6 + 1) * 64]
                            mm = pe.matmul(out.rearrange("p (m i) -> p m i", i=b), unit(k, u), rhs,
                                           start=True, stop=True)
                        mm.then_inc(lvl_mm, 1)
                        fill(1 if lv < 6 else 0)
                assert filled[0] == stages["modC"]["n"]
                mod_turn(g0 + 5)
                pe.wait_ge(lvl_k, 2 * LEVELS)
                pe.wait_ge(lvl_out, 4 * LEVELS)
                for h in range(HEADS_A + 1):
                    if h < HEADS_A:
                        if h >= 1:
                            pe.wait_ge(k_copied, h)
                        for j, (k, blk) in enumerate(((KFW, 0), (KFW, 1), (KBW, 0), (KBW, 2))):
                            mm = pe.transpose(bank[5][:, j * P:(j + 1) * P], k[:, h, blk * P:(blk + 1) * P], IDENT[:])
                        mm.then_inc(k_turned, 1)
                    g = h - 1
                    if g >= 0:
                        pe.wait_ge(k_copied, g + 1)
                        if g >= 2:
                            pe.wait_ge(st_ready, 4 * (g - 1))
                        for j, blk in enumerate((0, 1, 0, 2)):
                            mm = pe.matmul(bank[3 + g % 2][:, j * P:(j + 1) * P], KTOK[:, g % 2, j, :],
                                           VT[:, blk, g * P:(g + 1) * P], start=True, stop=True)
                        mm.then_inc(st_mm, 1)
                pe.wait_ge(mod_cols, first_group("modD"))
                def head_stat(h):
                    pe.wait_ge(o_copied, h + 1)
                    pe.matmul(cols3(bank[h]), ONES[:], SQ[:, h % 2, :], start=True, stop=True).then_inc(o_stat, 1)

                for h in range(HEADS_A):
                    pe.wait_ge(st_ready, 4 * h + 4)
                    O = bank[h]
                    for t in range(TOKS):
                        out = O[:, t * P:(t + 1) * P]
                        terms = [(VT[:, t, h * P:(h + 1) * P], ATT[:, TOKS * h + t, :])]
                        if t > 0:
                            first = (ST[:, h, :], KFW[:, h, P:2 * P])
                            last = (ST[:, 4 + h, :], KBW[:, h, P:2 * P])
                            terms.append((first[t - 1], QF[:, h, t * P:(t + 1) * P]))
                            terms.append((last[2 - t], QB[:, h, t * P:(t + 1) * P]))
                        for n, (l, r) in enumerate(terms):
                            mm = pe.matmul(out, l, r, start=(n == 0), stop=(n == len(terms) - 1))
                    mm.then_inc(o_mm, 1)
                    if h >= 1:
                        head_stat(h - 1)
                def cat_wait(kk):
                    pe.wait_ge(cat_ready, kk - 4 + 1 if kk >= 4 else 4 + kk + 1)

                steps = out_four(s, (4, 5, 6, 7, 0, 1, 2, 3), cat_wait)
                next(steps)
                head_stat(HEADS_A - 1)
                for _ in steps:
                    pass
                out_small(s)

            def odd(s):
                first_four(s)
                for tau in range(4, 24):
                    if tau >= 20:
                        pe.wait_ge(conv_step, 4 * (tau - 20) + 1)
                    elif tau >= 4:
                        pe.wait_ge(proj_out, 32 + tau - 3)
                    pe_half(pe, f"in{s}", tau, hh, hl, 8, cols3(bank[tau % 4]), True, True)
                mod_stage(MIDDLE[s])
                for _ in out_four(s, range(KD), lambda kk: pe.wait_ge(cat_ready, 8 + kk + 1)):
                    pass
                out_small(s)

            pe.sem_inc(silu_done, 2)
            pe.sem_inc(out_done, 4)
            pe.wait_ge(cond_ready, 1)
            pe.wait_ge(x_ready, 4)
            mod_stage("mod0")
            pre_stats(0)
            for s in range(upto):
                {"ffn": ffn, "even": even, "odd": odd}[SUBLAYERS[s][0]](s)
                post_stats(s)
                if s < upto - 1:
                    pe.wait_ge(out_done, 4 + 8 * (s + 1))
                    groups = between(s + 1)
                    for n in range(4 * len(groups)):
                        mod_slot(BETWEEN[s], n)
                    for g in groups[:-1]:
                        mod_turn(g)
                    pre_stats(s + 1)
                    mod_turn(groups[-1])
            for b in range(2):
                pe.wait_ge(x_ready, 4 * upto + 2 + 2 * b)
                for t in range(TOKS):
                    n = TOKS * b + t
                    if n >= 4:
                        pe.wait_ge(y_copied, n - 3)
                    for d in range(4):
                        mm = pe.transpose(bank[n % 4 + 4][:, d * P:(d + 1) * P],
                                          X[:, 4 * b + d, t * P:(t + 1) * P], IDENT[:])
                    mm.then_inc(tp_done, 1)


_INS = ['x_prompt', 'x_sample', 'c', 'state_hgrn', 'cache_k', 'cache_v', 'c_ctx', 'mod_w', 'mod_b', 'norm_pre',
        'norm_post', 'ffn_w_in', 'ffn_w_out', 'ab_w_in', 'ab_w_out', 'a_lb', 'a_gnorm', 'b_rpb', 'cv_w_in',
        'cv_conv', 'cv_w_out']
_OUTS = [(1, 128, 1024), (1, 256, 1024), (1, 1, 2, 4, 128, 128), (1, 1, 8, 128, 64), (1, 1, 8, 128, 64)]


def kernel(**inputs):
    import concourse.bacc as bacc
    from concourse.bass_utils import run_bass_kernel_spmd

    nc = bacc.Bacc("TRN2", target_bir_lowering=False, num_devices=1)
    arrays, args = {}, []
    given = {name: np.ascontiguousarray(inputs[name]) for name in _INS}
    given |= dict(zip(("identity", "level_masks", "window_mask", "flip_scaled"), constants()))
    for name, a in given.items():
        arrays[f"in_{name}"] = a
        args.append(nc.dram_tensor(f"in_{name}", a.shape, mybir.dt.from_np(a.dtype), kind="ExternalInput").ap())
    for i, shape in enumerate(_OUTS):
        args.append(nc.dram_tensor(f"out_{i}", shape, F32, kind="ExternalOutput").ap())
    trunk(nc, *args)
    r = run_bass_kernel_spmd(nc, [arrays], core_ids=[0])
    return tuple(r.results[0][f"out_{i}"] for i in range(len(_OUTS)))
```
